# Optimizing a Trainium2 kernel written in Bass

```python
import jax, jax.numpy as jnp
from jax import lax
import numpy as np
import math
import jax
import jax.numpy as jnp

D_MODEL = 1024
BATCH = 1
SEQ = 512
DEPTH = 2

CHUNK = 64
N_MIXERS = 2
N_CONV_LAYERS = (DEPTH + 1) // 2
N_SSD_LAYERS = DEPTH // 2
N_MOD = 6
EPS = 1e-6

SC_WIDTH = 3

M_EXPAND = 2
M_D_INNER = M_EXPAND * D_MODEL
M_HEAD_DIM = 64
M_N_HEADS = M_D_INNER // M_HEAD_DIM
M_N_GROUPS = 8
M_HEADS_PER_GROUP = M_N_HEADS // M_N_GROUPS
M_D_STATE = 128
M_CONV_WIDTH = 4
M_CONV_DIM = M_D_INNER + 2 * M_N_GROUPS * M_D_STATE
M_IN_DIM = M_D_INNER + M_CONV_DIM + M_N_HEADS
SSD_CHUNK = CHUNK

D_FF = -(-8 * D_MODEL // (3 * 256)) * 256


def rms_normalize(x):
    xf = x.astype(jnp.float32)
    xf = xf * lax.rsqrt(jnp.mean(xf * xf, axis=-1, keepdims=True) + EPS)
    return xf.astype(x.dtype)

def rmsnorm(x, g):
    return rms_normalize(x) * g

def causal_depthwise_conv(x, w):
    k_width = w.shape[0]
    s = x.shape[1]
    xp = jnp.pad(x, ((0, 0), (k_width - 1, 0), (0, 0)))
    y = w[0] * xp[:, 0:s]
    for k in range(1, k_width):
        y = y + w[k] * xp[:, k:k + s]
    return y

def short_conv_mixer(h, w_in, conv_w, w_out):
    b_gate, c_gate, v = jnp.split(h @ w_in, 3, axis=-1)
    u = causal_depthwise_conv(c_gate * v, conv_w)
    return (b_gate * u) @ w_out

def ssd_chunked(xh, dt, a, bm, cm):
    bsz, s, g, r, p = xh.shape
    n = bm.shape[-1]
    nc, l = s // SSD_CHUNK, SSD_CHUNK
    dtype = xh.dtype
    xdt = (xh * dt[..., None].astype(dtype)).reshape(bsz, nc, l, g, r, p)
    bm = bm.reshape(bsz, nc, l, g, n)
    cm = cm.reshape(bsz, nc, l, g, n)
    cs = jnp.cumsum((dt * a).reshape(bsz, nc, l, g, r), axis=2)
    causal = jnp.tril(jnp.ones((l, l), dtype=bool))[None, None, :, :, None, None]
    seg = cs[:, :, :, None] - cs[:, :, None]
    decay = jnp.exp(jnp.where(causal, seg, -jnp.inf)).astype(dtype)
    cb = jnp.einsum('bclgn,bcsgn->bclsg', cm, bm)
    y_diag = jnp.einsum('bclsgr,bcsgrp->bclgrp', cb[..., None] * decay, xdt)
    decay_to_end = jnp.exp(cs[:, :, -1:] - cs).astype(dtype)
    states = jnp.einsum('bclgn,bclgr,bclgrp->bcgrpn', bm, decay_to_end, xdt)
    chunk_decay = jnp.exp(cs[:, :, -1]).astype(dtype)

    def step(state, inp):
        st, dec = inp
        return state * dec[..., None, None] + st, state

    h0 = jnp.zeros((bsz, g, r, p, n), dtype)
    _, prev = lax.scan(step, h0, (jnp.moveaxis(states, 1, 0), jnp.moveaxis(chunk_decay, 1, 0)))
    prev = jnp.moveaxis(prev, 0, 1)
    y_off = jnp.einsum('bclgn,bcgrpn,bclgr->bclgrp', cm, prev, jnp.exp(cs).astype(dtype))
    return (y_diag + y_off).reshape(bsz, s, g, r, p)

def ssd_mixer(h, w_in, conv_w, conv_b, dt_bias, a_log, d_skip, norm_g, w_out):
    bsz, s, _ = h.shape
    g, r, p, n = M_N_GROUPS, M_HEADS_PER_GROUP, M_HEAD_DIM, M_D_STATE
    z, xbc, dt_raw = jnp.split(h @ w_in, [M_D_INNER, M_D_INNER + M_CONV_DIM], axis=-1)
    xbc = jax.nn.silu(causal_depthwise_conv(xbc, conv_w) + conv_b)
    xs, bm, cm = jnp.split(xbc, [M_D_INNER, M_D_INNER + g * n], axis=-1)
    xs = xs.reshape(bsz, s, g, r, p)
    bm = bm.reshape(bsz, s, g, n)
    cm = cm.reshape(bsz, s, g, n)
    dt = jax.nn.softplus(dt_raw.astype(jnp.float32) + dt_bias.astype(jnp.float32)).reshape(bsz, s, g, r)
    a = -jnp.exp(a_log.astype(jnp.float32)).reshape(g, r)
    y = ssd_chunked(xs, dt, a, bm, cm) + d_skip.reshape(g, r)[:, :, None] * xs
    y = y.reshape(bsz, s, M_D_INNER) * jax.nn.silu(z)
    y = rms_normalize(y.reshape(bsz, s, g, M_D_INNER // g)).reshape(bsz, s, M_D_INNER) * norm_g
    return y @ w_out

def swiglu_ffn(h, w_in, w_out):
    gate, up = jnp.split(h @ w_in, 2, axis=-1)
    return (jax.nn.silu(gate) * up) @ w_out

def first_inputs(seed: int = 0) -> dict:
    key = jax.random.key(seed)
    ks = jax.random.split(key, 20)
    f32 = jnp.float32
    nrm = lambda k, shape, scale: jax.random.normal(k, shape, f32) * scale
    dt_init = jnp.exp(jax.random.uniform(ks[11], (N_SSD_LAYERS, M_N_HEADS), f32,
                                         np.log(1e-3), np.log(1e-1)))
    return {
        "x": nrm(ks[0], (BATCH, SEQ, D_MODEL), 1.0),
        "c": nrm(ks[1], (BATCH, D_MODEL), 1.0),
        "ada_w": nrm(ks[2], (D_MODEL, DEPTH * N_MOD * D_MODEL), 0.5 * D_MODEL ** -0.5),
        "ada_b": nrm(ks[3], (DEPTH * N_MOD * D_MODEL,), 0.02),
        "norm_g": 1.0 + nrm(ks[4], (DEPTH, 4, D_MODEL), 0.02),
        "a_w_in": nrm(ks[5], (N_CONV_LAYERS, D_MODEL, 3 * D_MODEL), D_MODEL ** -0.5),
        "a_conv_w": nrm(ks[6], (N_CONV_LAYERS, SC_WIDTH, D_MODEL), SC_WIDTH ** -0.5),
        "a_w_out": nrm(ks[7], (N_CONV_LAYERS, D_MODEL, D_MODEL), D_MODEL ** -0.5),
        "m_w_in": nrm(ks[8], (N_SSD_LAYERS, D_MODEL, M_IN_DIM), D_MODEL ** -0.5),
        "m_conv_w": nrm(ks[9], (N_SSD_LAYERS, M_CONV_WIDTH, M_CONV_DIM), M_CONV_WIDTH ** -0.5),
        "m_conv_b": nrm(ks[10], (N_SSD_LAYERS, M_CONV_DIM), 0.02),
        "m_dt_bias": dt_init + jnp.log(-jnp.expm1(-dt_init)),
        "m_a_log": jnp.log(jax.random.uniform(ks[12], (N_SSD_LAYERS, M_N_HEADS), f32, 1.0, 16.0)),
        "m_d": 1.0 + nrm(ks[13], (N_SSD_LAYERS, M_N_HEADS), 0.1),
        "m_norm_g": 1.0 + nrm(ks[14], (N_SSD_LAYERS, M_D_INNER), 0.02),
        "m_w_out": nrm(ks[15], (N_SSD_LAYERS, M_D_INNER, D_MODEL), M_D_INNER ** -0.5),
        "f_w_in": nrm(ks[16], (DEPTH, D_MODEL, 2 * D_FF), D_MODEL ** -0.5),
        "f_w_out": nrm(ks[17], (DEPTH, D_FF, D_MODEL), D_FF ** -0.5),
    }

def first_block(x, c, ada_w, ada_b, norm_g, a_w_in, a_conv_w, a_w_out, m_w_in, m_conv_w,
              m_conv_b, m_dt_bias, m_a_log, m_d, m_norm_g, m_w_out, f_w_in, f_w_out):
    bsz = x.shape[0]
    mod = (jax.nn.silu(c) @ ada_w + ada_b).reshape(bsz, DEPTH, 2, 3, D_MODEL)
    for i in range(DEPTH):
        j = i // N_MIXERS
        shift, scale, gate = (mod[:, i, 0, k][:, None, :] for k in range(3))
        h = rmsnorm(x, norm_g[i, 0]) * (1.0 + scale) + shift
        if i % N_MIXERS == 0:
            y = short_conv_mixer(h, a_w_in[j], a_conv_w[j], a_w_out[j])
        else:
            y = ssd_mixer(h, m_w_in[j], m_conv_w[j], m_conv_b[j], m_dt_bias[j], m_a_log[j],
                          m_d[j], m_norm_g[j], m_w_out[j])
        x = x + gate * rmsnorm(y, norm_g[i, 1])
        shift, scale, gate = (mod[:, i, 1, k][:, None, :] for k in range(3))
        h = rmsnorm(x, norm_g[i, 2]) * (1.0 + scale) + shift
        y = swiglu_ffn(h, f_w_in[i], f_w_out[i])
        x = x + gate * rmsnorm(y, norm_g[i, 3])
    return x


DEPTH_2 = 1


ATTN_HEAD_DIM = 64
ATTN_WIDTH = D_MODEL // 2
ATTN_HEADS = ATTN_WIDTH // ATTN_HEAD_DIM
LEFT_CHUNKS = 8
BAND = (LEFT_CHUNKS + 1) * CHUNK
REL_CLIP = 128
N_REL = 2 * REL_CLIP + 1

DN_HEAD_DIM = 128
DN_WIDTH = D_MODEL - ATTN_WIDTH
DN_HEADS = DN_WIDTH // DN_HEAD_DIM
CONV_WIDTH = 4

MIX_WIDTH = ATTN_WIDTH + DN_WIDTH
IN_PROJ_WIDTH = 3 * ATTN_WIDTH + 4 * DN_WIDTH + 2 * DN_HEADS

PEER_HEADS = 8
PEER_KEY_DIM = 256
PEER_HALF = PEER_KEY_DIM // 2
N_KEYS = 128
N_EXPERTS = N_KEYS * N_KEYS
PEER_TOPK = 16
PEER_BLOCK = 128


def rms_norm(x, gain):
    xf = x.astype(jnp.float32)
    y = xf * lax.rsqrt(jnp.mean(xf * xf, axis=-1, keepdims=True) + EPS)
    return (y * gain.astype(jnp.float32)).astype(x.dtype)

def l2_norm(x):
    xf = x.astype(jnp.float32)
    return xf * lax.rsqrt(jnp.sum(xf * xf, axis=-1, keepdims=True) + EPS)

def modulate(h, shift, scale):
    return h * (1.0 + scale) + shift

def chunked_band_attention(q, k, v, q_gain, k_gain, rel_bias):
    B, S = q.shape[:2]
    nc = S // CHUNK
    shp = (B, nc, CHUNK, ATTN_HEADS, ATTN_HEAD_DIM)
    pad = ((0, 0), (LEFT_CHUNKS, 0), (0, 0), (0, 0), (0, 0))
    q = rms_norm(q, q_gain).reshape(shp)
    k = jnp.pad(rms_norm(k, k_gain).reshape(shp), pad)
    v = jnp.pad(v.reshape(shp), pad)
    band_idx = np.arange(nc)[:, None] + np.arange(LEFT_CHUNKS + 1)[None, :]
    kb = k[:, band_idx].reshape(B, nc, BAND, ATTN_HEADS, ATTN_HEAD_DIM)
    vb = v[:, band_idx].reshape(B, nc, BAND, ATTN_HEADS, ATTN_HEAD_DIM)
    scores = jnp.einsum("bnqhd,bnkhd->bhnqk", q, kb,
                        preferred_element_type=jnp.float32) * (ATTN_HEAD_DIM ** -0.5)
    rel = np.arange(CHUNK)[:, None] + LEFT_CHUNKS * CHUNK - np.arange(BAND)[None, :]
    rel_idx = np.clip(rel, -REL_CLIP, REL_CLIP) + REL_CLIP
    bias = rel_bias.astype(jnp.float32)[:, rel_idx]
    valid = (np.arange(nc)[:, None] + np.arange(BAND)[None, :] // CHUNK) >= LEFT_CHUNKS
    scores = jnp.where(valid[None, None, :, None, :], scores + bias[None, :, None], -jnp.inf)
    p = jax.nn.softmax(scores, axis=-1).astype(vb.dtype)
    o = jnp.einsum("bhnqk,bnkhd->bnqhd", p, vb)
    return o.reshape(B, S, ATTN_WIDTH)

def causal_depthwise_conv_2(x, w):
    S = x.shape[1]
    xp = jnp.pad(x, ((0, 0), (CONV_WIDTH - 1, 0), (0, 0)))
    y = xp[:, 0:S] * w[0]
    for i in range(1, CONV_WIDTH):
        y = y + xp[:, i:i + S] * w[i]
    return jax.nn.silu(y)

def gated_delta_rule(q, k, v, g, beta):
    B, S, H, Dk = q.shape
    Dv = v.shape[-1]
    nc = S // CHUNK

    def to_chunks(t):
        return t.astype(jnp.float32).reshape(B, nc, CHUNK, H, -1).transpose(1, 0, 3, 2, 4)

    q = to_chunks(q) * (Dk ** -0.5)
    k = to_chunks(k)
    v = to_chunks(v)
    g = g.astype(jnp.float32).reshape(B, nc, CHUNK, H).transpose(1, 0, 3, 2)
    beta = beta.astype(jnp.float32).reshape(B, nc, CHUNK, H).transpose(1, 0, 3, 2)
    gc = jnp.cumsum(g, axis=-1)
    tri = np.tril(np.ones((CHUNK, CHUNK), dtype=bool))
    strict = np.tril(np.ones((CHUNK, CHUNK), dtype=bool), -1)
    decay = jnp.exp(jnp.where(tri, gc[..., :, None] - gc[..., None, :], -jnp.inf))
    k_beta = k * beta[..., None]
    v_beta = v * beta[..., None]
    lower = jnp.where(strict, jnp.einsum("nbhid,nbhjd->nbhij", k_beta, k) * decay, 0.0)
    rhs = jnp.concatenate([v_beta, k_beta * jnp.exp(gc)[..., None]], axis=-1)
    sol = lax.linalg.triangular_solve(jnp.eye(CHUNK, dtype=jnp.float32) + lower, rhs,
                                      left_side=True, lower=True, unit_diagonal=True)
    u = sol[..., :Dv]
    w = sol[..., Dv:]
    intra = jnp.einsum("nbhid,nbhjd->nbhij", q, k) * decay

    def step(state, xs):
        q_c, k_c, u_c, w_c, a_c, g_c = xs
        v_new = u_c - jnp.einsum("bhcd,bhde->bhce", w_c, state)
        o = (jnp.einsum("bhcd,bhde->bhce", q_c * jnp.exp(g_c)[..., None], state)
             + jnp.einsum("bhij,bhje->bhie", a_c, v_new))
        g_last = g_c[..., -1]
        k_dec = k_c * jnp.exp(g_last[..., None] - g_c)[..., None]
        state = state * jnp.exp(g_last)[..., None, None] + jnp.einsum("bhcd,bhce->bhde", k_dec, v_new)
        return state, o

    state0 = jnp.zeros((B, H, Dk, Dv), jnp.float32)
    _, o = lax.scan(step, state0, (q, k, u, w, intra, gc))
    return o.transpose(1, 0, 3, 2, 4).reshape(B, S, H, Dv)

def peer(h, w_query, query_gain, sub_keys_1, sub_keys_2, expert_down, expert_up):
    B, S, D = h.shape
    n_blocks = (B * S) // PEER_BLOCK

    def block(hb):
        qry = (hb @ w_query).reshape(PEER_BLOCK, PEER_HEADS, PEER_KEY_DIM)
        qry = rms_norm(qry, query_gain)
        s1 = jnp.einsum("thd,nd->thn", qry[..., :PEER_HALF], sub_keys_1, preferred_element_type=jnp.float32)
        s2 = jnp.einsum("thd,nd->thn", qry[..., PEER_HALF:], sub_keys_2, preferred_element_type=jnp.float32)
        v1, i1 = lax.top_k(s1, PEER_TOPK)
        v2, i2 = lax.top_k(s2, PEER_TOPK)
        cand_s = (v1[..., :, None] + v2[..., None, :]).reshape(PEER_BLOCK, PEER_HEADS, PEER_TOPK * PEER_TOPK)
        cand_i = (i1[..., :, None] * N_KEYS + i2[..., None, :]).reshape(PEER_BLOCK, PEER_HEADS, PEER_TOPK * PEER_TOPK)
        top_s, pos = lax.top_k(cand_s, PEER_TOPK)
        experts = jnp.take_along_axis(cand_i, pos, axis=-1)
        gates = jax.nn.softmax(top_s, axis=-1)
        u = expert_down[experts]
        vv = expert_up[experts]
        act = jax.nn.gelu(jnp.einsum("thkd,td->thk", u, hb, preferred_element_type=jnp.float32),
                          approximate=False)
        return jnp.einsum("thk,thkd->td", (gates * act).astype(vv.dtype), vv)

    out = lax.map(block, h.reshape(n_blocks, PEER_BLOCK, D))
    return out.reshape(B, S, D)

def hybrid_layer(x, c, w_ada, b_ada, norm1_gain, w_in, attn_q_gain, attn_k_gain, attn_rel_bias,
                 attn_out_gain, dn_conv_w, dn_a_log, dn_dt_bias, dn_out_gain, w_out, norm2_gain,
                 peer_w_query, peer_query_gain, peer_sub_keys_1, peer_sub_keys_2,
                 peer_expert_down, peer_expert_up):
    B, S, _ = x.shape
    mod = jax.nn.silu(c) @ w_ada + b_ada
    shift1, scale1, gate1, shift2, scale2, gate2 = [m[:, None, :] for m in jnp.split(mod, 6, axis=-1)]

    h = modulate(rms_norm(x, norm1_gain), shift1, scale1)
    proj = h @ w_in
    cuts = [ATTN_WIDTH, 2 * ATTN_WIDTH, 3 * ATTN_WIDTH, 3 * ATTN_WIDTH + 3 * DN_WIDTH,
            3 * ATTN_WIDTH + 4 * DN_WIDTH, 3 * ATTN_WIDTH + 4 * DN_WIDTH + DN_HEADS]
    qa, ka, va, qkv_b, z_b, b_raw, a_raw = jnp.split(proj, cuts, axis=-1)

    hd_a = (B, S, ATTN_HEADS, ATTN_HEAD_DIM)
    o_a = chunked_band_attention(qa.reshape(hd_a), ka.reshape(hd_a), va.reshape(hd_a),
                                 attn_q_gain, attn_k_gain, attn_rel_bias)
    o_a = rms_norm(o_a, attn_out_gain)

    qkv_b = causal_depthwise_conv_2(qkv_b, dn_conv_w)
    q_b, k_b, v_b = jnp.split(qkv_b, 3, axis=-1)
    hd_b = (B, S, DN_HEADS, DN_HEAD_DIM)
    q_b = l2_norm(q_b.reshape(hd_b))
    k_b = l2_norm(k_b.reshape(hd_b))
    beta = jax.nn.sigmoid(b_raw.astype(jnp.float32))
    g = -jnp.exp(dn_a_log.astype(jnp.float32)) * jax.nn.softplus(
        a_raw.astype(jnp.float32) + dn_dt_bias.astype(jnp.float32))
    o_b = gated_delta_rule(q_b, k_b, v_b.reshape(hd_b), g, beta)
    o_b = rms_norm(o_b, dn_out_gain) * jax.nn.silu(z_b.reshape(hd_b).astype(jnp.float32))
    o_b = o_b.reshape(B, S, DN_WIDTH).astype(x.dtype)

    mix = jnp.concatenate([o_a, o_b], axis=-1) @ w_out
    x = x + gate1 * mix

    h2 = modulate(rms_norm(x, norm2_gain), shift2, scale2)
    y = peer(h2, peer_w_query, peer_query_gain, peer_sub_keys_1, peer_sub_keys_2,
             peer_expert_down, peer_expert_up)
    return x + gate2 * y

def second_inputs(seed: int = 0) -> dict:
    key = jax.random.key(seed)
    ks = iter(jax.random.split(key, 32))
    L = DEPTH_2

    def nrm(shape, scale):
        return scale * jax.random.normal(next(ks), shape, jnp.float32)

    def gain(shape):
        return 1.0 + nrm(shape, 0.02)

    x = nrm((BATCH, SEQ, D_MODEL), 1.0)
    c = nrm((BATCH, D_MODEL), 1.0)
    w_ada = nrm((L, D_MODEL, 6 * D_MODEL), 0.5 * D_MODEL ** -0.5)
    b_ada = nrm((L, 6 * D_MODEL), 0.02)
    norm1_gain = gain((L, D_MODEL))
    w_in = nrm((L, D_MODEL, IN_PROJ_WIDTH), D_MODEL ** -0.5)
    attn_q_gain = gain((L, ATTN_HEAD_DIM))
    attn_k_gain = gain((L, ATTN_HEAD_DIM))
    attn_rel_bias = nrm((L, ATTN_HEADS, N_REL), 0.5)
    attn_out_gain = gain((L, ATTN_WIDTH))
    dn_conv_w = nrm((L, CONV_WIDTH, 3 * DN_WIDTH), CONV_WIDTH ** -0.5)
    dn_a_log = jnp.log(jax.random.uniform(next(ks), (L, DN_HEADS), jnp.float32, 1.0, 16.0))
    dt = jnp.exp(jax.random.uniform(next(ks), (L, DN_HEADS), jnp.float32,
                                    math.log(1e-3), math.log(1e-1)))
    dn_dt_bias = dt + jnp.log(-jnp.expm1(-dt))
    dn_out_gain = gain((L, DN_HEAD_DIM))
    w_out = nrm((L, MIX_WIDTH, D_MODEL), MIX_WIDTH ** -0.5)
    norm2_gain = gain((L, D_MODEL))
    peer_w_query = nrm((L, D_MODEL, PEER_HEADS * PEER_KEY_DIM), D_MODEL ** -0.5)
    peer_query_gain = gain((L, PEER_KEY_DIM))
    peer_sub_keys_1 = nrm((L, N_KEYS, PEER_HALF), PEER_HALF ** -0.5)
    peer_sub_keys_2 = nrm((L, N_KEYS, PEER_HALF), PEER_HALF ** -0.5)
    peer_expert_down = nrm((L, N_EXPERTS, D_MODEL), D_MODEL ** -0.5)
    peer_expert_up = nrm((L, N_EXPERTS, D_MODEL), 0.5)
    return {"x": x, "c": c, "w_ada": w_ada, "b_ada": b_ada, "norm1_gain": norm1_gain,
            "w_in": w_in, "attn_q_gain": attn_q_gain, "attn_k_gain": attn_k_gain,
            "attn_rel_bias": attn_rel_bias, "attn_out_gain": attn_out_gain,
            "dn_conv_w": dn_conv_w, "dn_a_log": dn_a_log, "dn_dt_bias": dn_dt_bias,
            "dn_out_gain": dn_out_gain, "w_out": w_out, "norm2_gain": norm2_gain,
            "peer_w_query": peer_w_query, "peer_query_gain": peer_query_gain,
            "peer_sub_keys_1": peer_sub_keys_1, "peer_sub_keys_2": peer_sub_keys_2,
            "peer_expert_down": peer_expert_down, "peer_expert_up": peer_expert_up}

def second_block(x, c, w_ada, b_ada, norm1_gain, w_in, attn_q_gain, attn_k_gain, attn_rel_bias,
              attn_out_gain, dn_conv_w, dn_a_log, dn_dt_bias, dn_out_gain, w_out, norm2_gain,
              peer_w_query, peer_query_gain, peer_sub_keys_1, peer_sub_keys_2,
              peer_expert_down, peer_expert_up):
    for layer in range(DEPTH_2):
        x = hybrid_layer(x, c, w_ada[layer], b_ada[layer], norm1_gain[layer], w_in[layer],
                         attn_q_gain[layer], attn_k_gain[layer], attn_rel_bias[layer],
                         attn_out_gain[layer], dn_conv_w[layer], dn_a_log[layer], dn_dt_bias[layer],
                         dn_out_gain[layer], w_out[layer], norm2_gain[layer], peer_w_query[layer],
                         peer_query_gain[layer], peer_sub_keys_1[layer], peer_sub_keys_2[layer],
                         peer_expert_down[layer], peer_expert_up[layer])
    return x


def setup_inputs(seed=0):
    out = dict(first_inputs(seed))
    for name, value in second_inputs(seed + 1).items():
        if name != "x":
            out[name + "_2"] = value
    return out


def reference(
    x, c, ada_w, ada_b, norm_g, a_w_in, a_conv_w, a_w_out, m_w_in, m_conv_w, m_conv_b,
    m_dt_bias, m_a_log, m_d, m_norm_g, m_w_out, f_w_in, f_w_out, c_2, w_ada_2, b_ada_2,
    norm1_gain_2, w_in_2, attn_q_gain_2, attn_k_gain_2, attn_rel_bias_2, attn_out_gain_2,
    dn_conv_w_2, dn_a_log_2, dn_dt_bias_2, dn_out_gain_2, w_out_2, norm2_gain_2, peer_w_query_2,
    peer_query_gain_2, peer_sub_keys_1_2, peer_sub_keys_2_2, peer_expert_down_2,
    peer_expert_up_2,
):
    x = first_block(
        x, c, ada_w, ada_b, norm_g, a_w_in, a_conv_w, a_w_out, m_w_in, m_conv_w, m_conv_b,
        m_dt_bias, m_a_log, m_d, m_norm_g, m_w_out, f_w_in, f_w_out,
    )
    return second_block(
        x, c_2, w_ada_2, b_ada_2, norm1_gain_2, w_in_2, attn_q_gain_2, attn_k_gain_2,
        attn_rel_bias_2, attn_out_gain_2, dn_conv_w_2, dn_a_log_2, dn_dt_bias_2, dn_out_gain_2,
        w_out_2, norm2_gain_2, peer_w_query_2, peer_query_gain_2, peer_sub_keys_1_2,
        peer_sub_keys_2_2, peer_expert_down_2, peer_expert_up_2,
    )


_drawn_inputs = setup_inputs


def setup_inputs(seed=0):
    import zlib

    import numpy as np

    out = dict(_drawn_inputs(seed))
    spreads = {}
    factors = {'m_conv_b': 5.794,
     'm_d': 3.007,
     'm_norm_g': 21.043,
     'norm1_gain_2': 8.0,
     'attn_q_gain_2': 8.0,
     'attn_k_gain_2': 8.0,
     'attn_out_gain_2': 64.0,
     'dn_a_log_2': 3.987,
     'dn_dt_bias_2': 3.005,
     'dn_out_gain_2': 22.99,
     'norm2_gain_2': 42.302,
     'peer_query_gain_2': 41.256,
     'attn_rel_bias_2': 5.626}
    for name, (base, spread) in spreads.items():
        noise = np.random.default_rng([zlib.crc32(name.encode()), seed]).standard_normal(out[name].shape)
        drawn = base * np.exp(spread * noise) if base else spread * noise
        out[name] = jnp.asarray(drawn.astype(out[name].dtype))
    for name, factor in factors.items():
        out[name] = (out[name] * factor).astype(out[name].dtype)
    return out
```

```python
from contextlib import ExitStack

import concourse.bass as bass
from concourse import mybir

ALU = mybir.AluOpType
ACT = mybir.ActivationFunctionType
F32 = mybir.dt.float32
U32 = mybir.dt.uint32
I32 = mybir.dt.int32
AX_X = mybir.AxisListType.X

D = 1024
S = 512
KD = 8
FF = 2816
KF = 22
EPS = 1e-6
NSLAB = 3
SLAB = 4096
GRING = 12
GG = 4

_COLS = [("c", 8), ("adab", 96), ("ng", 64), ("acw", 24), ("mcw", 128), ("mcb", 32), ("mng", 16),
         ("md", 16), ("c2", 8), ("adab2", 48), ("n1", 8), ("n2", 8), ("aog", 4), ("qg", 1), ("kg", 1),
         ("dcw", 48), ("dog", 1), ("pqg", 2), ("mdt", 1), ("mal", 1), ("dal", 1), ("ddt", 1)]
COL = {}
_at = 0
for _n, _k in _COLS:
    COL[_n] = _at
    _at += _k
NCOL = _at
LEVELS = [1, 2, 4, 8, 16, 32, 64]
CIDENT, CTRI, CTRIS, CBLK, CONES, CGT, CLEV = 0, 1, 2, 3, 4, 5, 6
NCONST = 6 + len(LEVELS)


class Bank:

    def __init__(self, ap, sem=None):
        self.ap = ap
        self.sem = sem
        self.uses = 0
        self.free = []


class Ring:
    def __init__(self, banks):
        self.banks = banks
        self.n = 0

    def next(self):
        b = self.banks[self.n % len(self.banks)]
        self.n += 1
        return b


class Program:

    def __init__(self, nc, ctx):
        self.nc = nc
        self.ctx = ctx
        self.q = {e: [] for e in ("pe", "act", "dve", "pool", "sp")}
        self.sem = {e: ctx.enter_context(nc.semaphore("s_" + e)) for e in ("pe", "act", "dve", "pool")}
        self.n = {e: 0 for e in self.sem}
        self.nsem = 0
        self.stores = []

    def put(self, eng, fn, *waits, quiet=False):
        flat = []
        for w in waits:
            if w is None:
                continue
            flat.extend(w if isinstance(w, list) else [w])
        if quiet:
            self.q[eng].append((fn, flat, None, 0))
            return None
        self.n[eng] += 1
        self.q[eng].append((fn, flat, self.sem[eng], 1))
        return (self.sem[eng], self.n[eng])

    def new_sem(self):
        self.nsem += 1
        return self.ctx.enter_context(self.nc.semaphore(f"d{self.nsem}"))

    def dma(self, eng, out, in_, *waits, slot=None, store=False):
        if slot is None:
            slot = Bank(None, self.new_sem())
        slot.uses += 1
        flat = []
        for w in waits:
            if w is not None:
                flat.extend(w if isinstance(w, list) else [w])
        self.q[eng].append((lambda e: e.dma_start(out, in_), flat, slot.sem, 16))
        tok = (slot.sem, 16 * slot.uses)
        if store:
            self.stores.append(tok)
        return tok

    def replay(self, eng, e):
        seen = {}
        for fn, waits, sem, inc in self.q[eng]:
            need = {}
            for s, v in waits:
                need[s.name] = (s, max(v, need.get(s.name, (s, 0))[1]))
            for name, (s, v) in need.items():
                if seen.get(name, 0) < v:
                    e.wait_ge(s, v)
                    seen[name] = v
            ins = fn(e)
            if sem is not None:
                ins.then_inc(sem, inc)


def build(nc, t, out):
    ctx = ExitStack()
    with ctx:
        P = Program(nc, ctx)
        put = P.put

        arena = ctx.enter_context(nc.sbuf_tensor("arena", [128, 53000], F32))
        psum = ctx.enter_context(nc.psum_tensor("psum", [128, 8, 512], F32))
        at = [0]

        def take(n):
            a = at[0]
            at[0] += n
            assert at[0] <= 53000, at[0]
            return arena[:, a:a + n]

        const = take(NCONST * 128).rearrange("p (a n) -> p a n", n=128)
        col = take(NCOL)
        mod = take(144)
        der = take(160)
        csil = take(16)
        xT = take(4096).rearrange("p (k n) -> p k n", k=8)
        hT = take(4096).rearrange("p (k n) -> p k n", k=8)
        slabs = Ring([Bank(take(SLAB), P.new_sem()) for _ in range(NSLAB)])
        tmp = Ring([Bank(take(512)) for _ in range(8)])
        rst = Ring([Bank(take(512)) for _ in range(2)])
        BASE = at[0]

        banks = [Bank(psum[:, i, :]) for i in range(8)]
        ring = Ring(banks)

        def cc(name, i=0, n=1):
            a = COL[name] + i
            return col[:, a:a + n]

        ident = const[:, CIDENT, :]
        tri = const[:, CTRI, :]
        tris = const[:, CTRIS, :]
        blk = const[:, CBLK, :]
        ones = const[:, CONES, :]
        gt_ = const[:, CGT, :]

        def mm(o, pairs, *waits, start=True, stop=True, skip=False):
            n = len(pairs)
            for i, (a, b) in enumerate(pairs):
                def f(e, a=a, b=b, i=i):
                    return e.matmul(o, a, b, start=start and i == 0, stop=stop and i == n - 1,
                                    skip_group_check=skip)
                tok = put("pe", f, *(waits if i == 0 else ()), quiet=i < n - 1)
            return tok

        def tr(o, i_, p, *waits):
            return put("pe", lambda e: e.transpose(o, i_, ident[0:p, 0:p]), *waits)

        def act(o, i_, func, *waits, bias=0.0, scale=1.0, accum=None):
            def f(e):
                k = {} if accum is None else {"accum_out": accum}
                return e.activation(o, i_, func, bias=bias, scale=scale, **k)
            return put("act", f, *waits)

        def tt(o, a, b, op, *waits, eng="dve"):
            return put(eng, lambda e: e.tensor_tensor(o, a, b, op), *waits)

        def ts(o, a, s1, op0, *waits, s2=None, op1=None, eng="dve"):
            def f(e):
                if op1 is None:
                    return e.tensor_scalar(o, a, s1, None, op0)
                return e.tensor_scalar(o, a, s1, s2, op0, op1)
            return put(eng, f, *waits)

        def stt(o, a, s, b, op0, op1, *waits):
            return put("dve", lambda e: e.scalar_tensor_tensor(out=o, in0=a, scalar=s, in1=b, op0=op0, op1=op1),
                       *waits)

        def vmax(o, i_, *waits):
            return put("dve", lambda e: e.max(o, i_), *waits)

        def vindex(o, m, i_, *waits):
            return put("dve", lambda e: e.max_index(o, m, i_), *waits)

        def vdrop(o, m, i_, *waits):
            return put("dve", lambda e: e.match_replace(o, m, i_, -3.0e38), *waits)

        def vcopy(o, i_, *waits):
            return put("dve", lambda e: e.tensor_copy(o, i_), *waits)

        def recip(o, i_, *waits):
            return put("dve", lambda e: e.reciprocal(o, i_), *waits)

        def red(o, i_, op, *waits):
            return put("dve", lambda e: e.tensor_reduce(o, i_, AX_X, op), *waits)

        def slab(src, k=8, w=512):
            b = slabs.next()
            dst = b.ap[:, 0:k * w]
            tok = P.dma("sp", dst, src, b.free, slot=b)
            return b, dst.rearrange("p (k n) -> p k n", k=k), tok

        t_col = P.dma("act", col, t["cols"])
        t_const = P.dma("act", const.rearrange("p a n -> p (a n)"), t["consts"])
        t_x0 = P.dma("act", xT.rearrange("p k n -> p (k n)"), t["xT"])
        xtok = [[t_x0] for _ in range(8)]

        t_c = act(csil[:, 0:8], cc("c", 0, 8), ACT.Silu, t_col)
        t_c = act(csil[:, 8:16], cc("c2", 0, 8), ACT.Silu, t_col)
        mod_tok = [None] * 36
        pending = list(range(36))

        def mod_slab(j):
            src = t["ada"][j] if j < 24 else t["ada2"][j - 24]
            b, w, tw = slab(src)
            bank = ring.next()
            c0 = 0 if j < 24 else 8
            for m in range(4):
                tok = mm(bank.ap[:, m:m + 1],
                         [(w[:, k, m * 128:(m + 1) * 128], csil[:, c0 + k:c0 + k + 1]) for k in range(8)],
                         tw, t_c, bank.free)
            b.free = [tok]
            o = 4 * j
            bias = cc("adab", o, 4) if j < 24 else cc("adab2", o - 96, 4)
            mod_tok[j] = tt(mod[:, o:o + 4], bank.ap[:, 0:4], bias, ALU.add, tok, t_col)
            bank.free = [mod_tok[j]]

        def mods(n):
            for _ in range(n):
                if pending:
                    mod_slab(pending.pop(0))

        def mods_until(j):
            while pending and pending[0] <= j:
                mod_slab(pending.pop(0))

        def derived(i):
            j0 = 6 * i
            mods_until(j0 + 5)
            o = 24 * i
            if i < 4:
                g_pre, g_post = cc("ng", 16 * i, 8), cc("ng", 16 * i + 8, 8)
            else:
                g_pre, g_post = cc("n1" if i == 4 else "n2", 0, 8), None
            a = stt(der[:, o:o + 8], mod[:, o + 8:o + 16], 1.0, g_pre, ALU.add, ALU.mult,
                    mod_tok[j0:j0 + 4], t_col)
            if g_post is not None:
                b = tt(der[:, o + 8:o + 16], mod[:, o + 16:o + 24], g_post, ALU.mult,
                       mod_tok[j0 + 4:j0 + 6], t_col)
            else:
                b = vcopy(der[:, o + 8:o + 16], mod[:, o + 16:o + 24], mod_tok[j0 + 4:j0 + 6])
            return a, b

        def shift(i, k):
            return mod[:, 24 * i + k:24 * i + k + 1]

        def pre(i, k):
            return der[:, 24 * i + k:24 * i + k + 1]

        def post(i, k):
            return der[:, 24 * i + 8 + k:24 * i + 9 + k]

        def sq_stat(bank, src, k, n, mat, *waits):
            b = tmp.next()
            t1 = act(b.ap, src, ACT.Square, b.free, *waits)
            t2 = mm(bank.ap, [(mat, b.ap)], t1, t_const, bank.free if k == 0 else None,
                    start=k == 0, stop=k == n - 1)
            b.free = [t2]
            return t1, t2

        def rstd(bank, tok, n, dst=None, dfree=None):
            if dst is None:
                r = rst.next()
                dst, dfree = r.ap, r.free
            else:
                r = None
            t0 = ts(dst, bank.ap, 1.0 / n, ALU.mult, tok, dfree, s2=EPS, op1=ALU.add)
            bank.free = [t0]
            t1 = act(dst, dst, ACT.Ln, t0)
            t2 = act(dst, dst, ACT.Exp, t1, scale=-0.5)
            return r, dst, t2

        h_free = [[] for _ in range(8)]

        def pre_norm(i, t_sh):
            bank = ring.next()
            for k in range(8):
                _, tok = sq_stat(bank, xT[:, k, :], k, 8, ones, xtok[k])
            r, ra, tr_ = rstd(bank, tok, D)
            toks = []
            for k in range(8):
                t1 = stt(hT[:, k, :], xT[:, k, :], pre(i, k), ra, ALU.mult, ALU.mult, tr_, t_sh, xtok[k], h_free[k])
                t2 = act(hT[:, k, :], hT[:, k, :], ACT.Identity, t1, bias=shift(i, k))
                toks.append(t2)
            r.free = [t1]
            return toks

        def out_proj(src_slabs, rhs, rhs_tok, yT, evac_free, norm=True, half=None, t_post=None):
            stat = banks[7]
            pend = None
            for g in range(2):
                bs = [ring.next() for _ in range(4)]
                for si, (src, k0, nk) in enumerate(src_slabs[g]):
                    b, w, tw = slab(src, nk)
                    last = si == len(src_slabs[g]) - 1
                    for m in range(4):
                        tok = mm(bs[m].ap, [(w[:, k, m * 128:(m + 1) * 128], rhs(k0 + k)) for k in range(nk)],
                                 tw, rhs_tok[k0:k0 + nk], bs[m].free if si == 0 else None,
                                 start=si == 0, stop=last)
                        if last:
                            kk = 4 * g + m
                            if norm:
                                t1 = act(yT[:, kk, :], bs[m].ap, ACT.Copy, tok, evac_free[kk])
                                sb = tmp.next()
                                t2 = act(sb.ap, bs[m].ap, ACT.Square, sb.free, tok)
                                bs[m].free = [t1, t2]
                                if pend is not None:
                                    pend()

                                def pend(kk=kk, sb=sb, t2=t2):
                                    t3 = mm(stat.ap, [(ones, sb.ap)], t2, stat.free if kk == 0 else None,
                                            start=kk == 0, stop=kk == 7)
                                    sb.free = [t3]
                                    return t3
                                ytok[kk] = t1
                            else:
                                t1 = stt(xT[:, kk, :], bs[m].ap, post(half, kk), xT[:, kk, :], ALU.mult, ALU.add,
                                         tok, t_post, xtok[kk])
                                bs[m].free = [t1]
                                xtok[kk] = [t1]
                    b.free = [tok]
                mods(1)
            if norm:
                tok = pend()
                r, ra, tr_ = rstd(stat, tok, D)
                for k in range(8):
                    b = tmp.next()
                    t1 = stt(b.ap, yT[:, k, :], post(half, k), ra, ALU.mult, ALU.mult, tr_, t_post, ytok[k], b.free)
                    t2 = tt(xT[:, k, :], xT[:, k, :], b.ap, ALU.add, t1, xtok[k])
                    b.free = [t2]
                    xtok[k] = [t2]
                r.free = [t1]
            return tok

        ytok = [None] * 8
        ring7 = Ring(banks[0:7])
        y_free = [[] for _ in range(8)]

        region_free = []

        def ffn(layer, half):
            nonlocal ring
            at[0] = BASE
            aT = take(KF * 512).rearrange("p (k n) -> p k n", k=KF)
            t_pre, t_post = derived(half)
            ht = pre_norm(half, t_pre)
            atok = [None] * KF
            for j in range(11):
                b, w, tw = slab(t["fin"][layer, j])
                for m in range(2):
                    kk = 2 * j + m
                    bg, bu = ring.next(), ring.next()
                    tg = mm(bg.ap, [(w[:, k, m * 128:(m + 1) * 128], hT[:, k, :]) for k in range(8)],
                            tw, ht, bg.free)
                    tu = mm(bu.ap, [(w[:, k, 256 + m * 128:256 + (m + 1) * 128], hT[:, k, :]) for k in range(8)],
                            bu.free)
                    sb = tmp.next()
                    t1 = act(sb.ap, bg.ap, ACT.Silu, tg, sb.free)
                    bg.free = [t1]
                    t2 = tt(aT[:, kk, :], bu.ap, sb.ap, ALU.mult, tu, t1, region_free)
                    bu.free = [t2]
                    sb.free = [t2]
                    atok[kk] = t2
                b.free = [tu]
                if j % 2 == 1:
                    mods(1)
            for k in range(8):
                h_free[k] = [tu]
            ring_keep = ring
            ring = ring7
            kg = [(0, 8), (8, 8), (16, 6)]
            tok = out_proj([[(t["fout"][layer, g, :, k0 * 512:(k0 + nk) * 512], k0, nk) for k0, nk in kg]
                            for g in range(2)], lambda k: aT[:, k, :], atok, hT, [[tu]] * 8, True, half, t_post)
            ring = ring_keep
            for k in range(8):
                h_free[k] = list(xtok[k])
            region_free[:] = [tok]

        def conv_mixer():
            nonlocal ring
            at[0] = BASE
            uT = take(4096).rearrange("p (k n) -> p k n", k=8)
            vT = take(4096).rearrange("p (k n) -> p k n", k=8)
            t_pre, t_post = derived(0)
            ht = pre_norm(0, t_pre)
            vt = [None] * 8
            ut = [None] * 8
            for j in range(6):
                b, w, tw = slab(t["ain"][j])
                for m in range(4):
                    kk = 4 * (j % 2) + m
                    bk = ring.next()
                    tok = mm(bk.ap, [(w[:, k, m * 128:(m + 1) * 128], hT[:, k, :]) for k in range(8)],
                             tw, ht, bk.free)
                    if j < 2:
                        vt[kk] = act(vT[:, kk, :], bk.ap, ACT.Copy, tok)
                        bk.free = [vt[kk]]
                    elif j < 4:
                        vt[kk] = tt(vT[:, kk, :], bk.ap, vT[:, kk, :], ALU.mult, tok, vt[kk])
                        bk.free = [vt[kk]]
                        cw = COL["acw"]
                        t1 = act(uT[:, kk, :], vT[:, kk, :], ACT.Copy, vt[kk], t_col,
                                 scale=col[:, cw + 16 + kk:cw + 17 + kk])
                        for tap, d in ((1, 1), (0, 2)):
                            t1 = stt(uT[:, kk, d:512], vT[:, kk, 0:512 - d], col[:, cw + 8 * tap + kk:cw + 8 * tap + kk + 1],
                                     uT[:, kk, d:512], ALU.mult, ALU.add, t1)
                        ut[kk] = t1
                    else:
                        ut[kk] = tt(uT[:, kk, :], bk.ap, uT[:, kk, :], ALU.mult, tok, ut[kk])
                        bk.free = [ut[kk]]
                b.free = [tok]
                mods(1)
            ring_keep = ring
            ring = ring7
            tok2 = out_proj([[(t["aout"][g], 0, 8)] for g in range(2)], lambda k: uT[:, k, :], ut, hT,
                            [[tok]] * 8, True, 0, t_post)
            ring = ring_keep
            for k in range(8):
                h_free[k] = list(xtok[k])
            region_free[:] = [tok2]

        def conv4(src_bank, dst, wcol, kk, ncol, tok, *waits, bias=None):
            w = lambda tap: col[:, wcol + ncol * tap + kk:wcol + ncol * tap + kk + 1]
            sb = tmp.next()
            if bias is None:
                t1 = act(sb.ap, src_bank.ap, ACT.Copy, tok, sb.free, scale=w(3))
            else:
                t1 = act(sb.ap, src_bank.ap, ACT.Identity, tok, sb.free, scale=w(3), bias=bias)
            for tap, d in ((2, 1), (1, 2), (0, 3)):
                t1 = stt(sb.ap[:, d:512], src_bank.ap[:, 0:512 - d], w(tap), sb.ap[:, d:512], ALU.mult, ALU.add, t1)
            src_bank.free = [t1]
            t2 = act(dst, sb.ap, ACT.Silu, t1, *waits)
            sb.free = [t2]
            return t2

        def softplus(dst, tmp3, *waits):
            e, u, v = tmp3
            t1 = act(e, dst, ACT.Abs, *waits)
            t2 = act(e, e, ACT.Exp, t1, scale=-1.0)
            t3 = ts(u, e, 2.0, ALU.add, t2)
            t4 = recip(u, u, t3)
            t5 = tt(e, e, u, ALU.mult, t4)
            t6 = tt(u, e, e, ALU.mult, t5)
            t7 = ts(v, u, 1.0 / 17.0, ALU.mult, t6)
            for n in (15, 13, 11, 9, 7, 5, 3):
                t7 = stt(v, v, 1.0 / n, u, ALU.add, ALU.mult, t7)
            t8 = stt(v, v, 1.0, e, ALU.add, ALU.mult, t7)
            t9 = ts(v, v, 2.0, ALU.mult, t8)
            return stt(dst, dst, 0.0, v, ALU.max, ALU.add, t9)

        def ssd_mixer():
            nonlocal ring
            at[0] = BASE
            xs = take(16 * 512).rearrange("p (k n) -> p k n", k=16)
            BT = take(8 * 512).rearrange("p (k n) -> p k n", k=8)
            CT = take(8 * 512).rearrange("p (k n) -> p k n", k=8)
            dtT = take(512)[0:32, :]
            daT = take(512)[0:32, :]
            sp3 = [tmp.next() for _ in range(3)]
            dttok = take(128).rearrange("p (c h) -> p c h", c=4)
            datok = take(128).rearrange("p (c h) -> p c h", c=4)
            cstok = take(128).rearrange("p (c h) -> p c h", c=4)
            wtok = take(128).rearrange("p (c h) -> p c h", c=4)
            cdec = take(128).rearrange("p (c h) -> p c h", c=4)
            nega = take(1)
            segb = [Bank(take(512)) for _ in range(2)]
            ceb = [Bank(take(512)) for _ in range(2)]
            cbm = [Bank(take(128)) for _ in range(2)]
            xdt = [Bank(take(256)) for _ in range(2)]
            xw = [Bank(take(256)) for _ in range(2)]
            btk = [Bank(take(128)) for _ in range(2)]
            st = [Bank(take(256)) for _ in range(2)]
            t_pre, t_post = derived(2)
            ht = pre_norm(2, t_pre)

            b, w, tw = slab(t["mdt"], 8, 32)
            bk = ring.next()
            tok = mm(bk.ap[0:32, :], [(w[:, k, :], hT[:, k, :]) for k in range(8)], tw, ht, bk.free)
            b.free = [tok]
            t1 = act(dtT, bk.ap[0:32, :], ACT.Identity, tok, region_free, bias=cc("mdt")[0:32, :])
            bk.free = [t1]
            ta = act(nega[0:32, :], cc("mal")[0:32, :], ACT.Exp, region_free, t_col)
            ta = ts(nega[0:32, :], nega[0:32, :], -1.0, ALU.mult, ta)
            t2 = softplus(dtT, [s.ap[0:32, :] for s in sp3], t1, *[s.free for s in sp3])
            for s in sp3:
                s.free = [t2]
            t3 = ts(daT, dtT, nega[0:32, 0:1], ALU.mult, t2, ta, region_free)
            bk = ring.next()
            bk2 = ring.next()
            for c in range(4):
                q1 = tr(bk.ap[:, 32 * c:32 * c + 32], dtT[:, 128 * c:128 * c + 128], 32, t2, bk.free, t_const)
                q2 = tr(bk2.ap[:, 32 * c:32 * c + 32], daT[:, 128 * c:128 * c + 128], 32, t3, bk2.free)
            flat = lambda a: a.rearrange("p c h -> p (c h)")
            d1 = act(flat(dttok), bk.ap[:, 0:128], ACT.Copy, q1, region_free)
            d2 = act(flat(datok), bk2.ap[:, 0:128], ACT.Copy, q2, region_free)
            bk.free, bk2.free = [d1], [d2]
            b1, b2 = ring.next(), ring.next()
            q1 = mm(b1.ap[:, 0:128], [(tri, flat(datok))], d2, b1.free)
            q2 = mm(b2.ap[:, 0:128], [(ones, flat(datok))], d2, b2.free)
            q2 = mm(b2.ap[:, 128:256], [(gt_, flat(datok))])
            d3 = act(flat(cstok), b1.ap[:, 0:128], ACT.Copy, q1, region_free)
            d5 = act(flat(cdec), b2.ap[:, 0:128], ACT.Exp, q2, region_free)
            d4 = act(flat(wtok), b2.ap[:, 128:256], ACT.Exp, q2, region_free)
            b1.free, b2.free = [d3], [d4]

            tk = {}
            for j in range(8):
                b, w, tw = slab(t["mxbc"][j])
                for m in range(4):
                    n = 4 * j + m
                    dst, ct = (BT[:, n, :], 16 + n) if n < 8 else (CT[:, n - 8, :], 16 + n) if n < 16 else (xs[:, n - 16, :], n - 16)
                    bk = ring.next()
                    tok = mm(bk.ap, [(w[:, k, m * 128:(m + 1) * 128], hT[:, k, :]) for k in range(8)],
                             tw, ht, bk.free)
                    tk[n] = conv4(bk, dst, COL["mcw"], ct, 32, tok, region_free, bias=cc("mcb", ct))
                b.free = [tok]
                if j % 2:
                    mods(1)

            yb = [[banks[0], banks[1]], [banks[2], banks[3]]]
            rg = Ring(banks[4:8])
            state = {}
            its = [(g, c) for g in range(8) for c in range(4)]

            def stage_a(n):
                g, c = its[n]
                p = n % 2
                cs = slice(128 * c, 128 * c + 128)
                s = {}
                b1, b2 = rg.next(), rg.next()
                q1 = mm(b1.ap[:, 0:128], [(BT[:, g, cs], CT[:, g, cs])], tk[g], tk[8 + g], b1.free)
                for r in range(4):
                    q2 = mm(b2.ap[:, 128 * r:128 * r + 128],
                            [(datok[:, c, 4 * g + r:4 * g + r + 1].broadcast_to([128, 128]), tri)], d2, b2.free)
                q3 = tr(b1.ap[:, 128:256], BT[:, g, cs], 128, q1)
                for u in range(2):
                    q4 = tr(b1.ap[:, 256 + 128 * u:384 + 128 * u], xs[:, 2 * g + u, cs], 128, tk[16 + 2 * g + u])
                s["cbm"] = tt(cbm[p].ap, b1.ap[:, 0:128], tri, ALU.mult, q4, cbm[p].free)
                v = segb[p].ap.rearrange("p (r n) -> p r n", r=4)
                hs = slice(4 * g, 4 * g + 4)
                t1 = tt(v, b2.ap.rearrange("p (r n) -> p r n", r=4),
                        cstok[:, c, hs].unsqueeze(2).broadcast_to([128, 4, 128]), ALU.subtract, q2, d3, segb[p].free)
                t2 = ts(segb[p].ap, segb[p].ap, 0.0, ALU.min, t1)
                t3 = act(ceb[p].ap, b2.ap, ACT.Exp, q2, t1, ceb[p].free)
                b2.free = [t1, t3]
                s["e"] = act(segb[p].ap, segb[p].ap, ACT.Exp, t2)
                x4 = xdt[p].ap.rearrange("p (r n) -> p r n", r=4)
                s["xdt"] = tt(x4, b1.ap[:, 256:512].rearrange("p (r n) -> p r n", r=4),
                              dttok[:, c, hs].unsqueeze(2).broadcast_to([128, 4, 64]), ALU.mult, q4, d1, xdt[p].free)
                s["btk"] = act(btk[p].ap, b1.ap[:, 128:256], ACT.Copy, q3, s["xdt"], btk[p].free)
                b1.free = [s["cbm"], s["xdt"], s["btk"]]
                ce = ceb[p].ap.rearrange("p (r n) -> p r n", r=4)
                if c:
                    s["ce"] = tt(ce, ce, CT[:, g, cs].unsqueeze(1).broadcast_to([128, 4, 128]), ALU.mult, t3)
                if c < 3:
                    xwv = xw[p].ap.rearrange("p (r n) -> p r n", r=4)
                    s["xw"] = tt(xwv, x4, wtok[:, c, hs].unsqueeze(2).broadcast_to([128, 4, 64]), ALU.mult,
                                 s["xdt"], d4, xw[p].free, eng="pool")
                else:
                    s["xw"] = None
                state[n] = s

            def stage_b(n):
                g, c = its[n]
                p = n % 2
                s = state.pop(n)
                cs = slice(128 * c, 128 * c + 128)
                v = segb[p].ap.rearrange("p (r n) -> p r n", r=4)
                tg = tt(v, v, cbm[p].ap.unsqueeze(1).broadcast_to([128, 4, 128]), ALU.mult, s["e"], s["cbm"])
                cbm[p].free = [tg]
                prev = st[g % 2]
                y = yb[g % 2]
                for r in range(4):
                    u, o = r // 2, 64 * (r % 2)
                    pairs = [(xdt[p].ap[:, 64 * r:64 * r + 64], v[:, r, :])]
                    if c:
                        pairs.append((prev.ap[:, 64 * r:64 * r + 64], ceb[p].ap[:, 128 * r:128 * r + 128]))
                    q = mm(y[u].ap[o:o + 64, cs], pairs, tg, s["xdt"], s.get("ce"), prev.tok if c else None,
                           y[u].free if c == 0 else None)
                segb[p].free = [q]
                ceb[p].free = [q]
                xdt[p].free = [q, s["xw"]] if s["xw"] else [q]
                if c == 0:
                    btkw = prev.free
                if c < 3:
                    b3 = rg.next()
                    q2 = mm(b3.ap[:, 0:256], [(btk[p].ap, xw[p].ap)], s["btk"], s["xw"], b3.free)
                    xw[p].free = [q2]
                    btk[p].free = [q2]
                    pv = prev.ap.rearrange("p (r n) -> p r n", r=4)
                    if c == 0:
                        prev.tok = act(prev.ap, b3.ap[:, 0:256], ACT.Copy, q2, btkw)
                    else:
                        t1 = tt(pv, pv, cdec[:, c, 4 * g:4 * g + 4].unsqueeze(2).broadcast_to([128, 4, 64]), ALU.mult,
                                d5, prev.tok, q)
                        prev.tok = tt(prev.ap, b3.ap[:, 0:256], prev.ap, ALU.add, q2, t1)
                    b3.free = [prev.tok]
                else:
                    btk[p].free = [s["btk"]]
                    prev.free = [q]
                    for u in range(2):
                        kk = 2 * g + u
                        tk[16 + kk] = stt(xs[:, kk, :], xs[:, kk, :], cc("md", kk), y[u].ap, ALU.mult, ALU.add, q, tk[16 + kk])
                        y[u].free = [tk[16 + kk]]

            for n in range(len(its) + 1):
                if n < len(its):
                    stage_a(n)
                if n:
                    stage_b(n - 1)

            mods(1)
            gt = [None] * 16
            for j in range(4):
                b, w, tw = slab(t["mz"][j])
                for m in range(4):
                    kk = 4 * j + m
                    bk = ring.next()
                    tok = mm(bk.ap, [(w[:, k, m * 128:(m + 1) * 128], hT[:, k, :]) for k in range(8)], tw, ht, bk.free)
                    sb = tmp.next()
                    t1 = act(sb.ap, bk.ap, ACT.Silu, tok, sb.free)
                    bk.free = [t1]
                    gt[kk] = tt(xs[:, kk, :], xs[:, kk, :], sb.ap, ALU.mult, t1, tk[16 + kk])
                    sb.free = [gt[kk]]
                b.free = [tok]
                for g in (2 * j, 2 * j + 1):
                    bk = ring.next()
                    for u in range(2):
                        _, tq = sq_stat(bk, xs[:, 2 * g + u, :], u, 2, ones, gt[2 * g + u])
                    r, ra, tr_ = rstd(bk, tq, 256)
                    for u in range(2):
                        kk = 2 * g + u
                        gt[kk] = stt(xs[:, kk, :], xs[:, kk, :], cc("mng", kk), ra, ALU.mult, ALU.mult, tr_, gt[kk])
                    r.free = [gt[kk]]
            ring_keep = ring
            ring = ring7
            tok2 = out_proj([[(t["mout"][g, :, k0 * 512:(k0 + 8) * 512], k0, 8) for k0 in (0, 8)] for g in range(2)],
                            lambda k: xs[:, k, :], gt, hT, [[tok]] * 8, True, 2, t_post)
            ring = ring_keep
            for k in range(8):
                h_free[k] = list(xtok[k])
            region_free[:] = [tok2]

        def hybrid():
            nonlocal ring
            at[0] = BASE
            t_pre, t_post = derived(4)
            ht = pre_norm(4, t_pre)
            mix = take(4096).rearrange("p (k n) -> p k n", k=8)
            mark = at[0]
            qT = take(2048).rearrange("p (k n) -> p k n", k=4)
            kT = take(2048).rearrange("p (k n) -> p k n", k=4)
            vtok = take(2048).rearrange("p (k n) -> p k n", k=4)
            T = take(4096).rearrange("p (h n) -> p h n", h=8)
            Sb = [Bank(take(512)) for _ in range(3)]
            PT = [Bank(take(2048).rearrange("p (j n) -> p j n", j=4)) for _ in range(2)]
            sm = [Bank(take(4)) for _ in range(4)]
            t_T = P.dma("act", T.rearrange("p h n -> p (h n)"), t["relT"], region_free)
            t_T = put("dve", lambda e: e.memset(T[0:64, :, 448:512], -3.0e38), t_T)

            def rows(bk, tok, kk, dst, gain):
                t0 = act(dst, bk.ap, ACT.Copy, tok, region_free)
                bk2 = ring.next()
                sb = tmp.next()
                t1 = act(sb.ap, bk.ap, ACT.Square, sb.free, tok)
                bk.free = [t0, t1]
                t2 = mm(bk2.ap, [(blk, sb.ap)], t1, bk2.free)
                sb.free = [t2]
                r, ra, tr_ = rstd(bk2, t2, 64)
                t3 = stt(dst, dst, gain, ra, ALU.mult, ALU.mult, tr_, t0)
                r.free = [t3]
                return t3

            qt, kt = [None] * 4, [None] * 4
            for j, (dst, toks, gain) in enumerate(((qT, qt, cc("qg")), (kT, kt, cc("kg")))):
                b, w, tw = slab(t["win2"][j])
                for m in range(4):
                    bk = ring.next()
                    tok = mm(bk.ap, [(w[:, k, m * 128:(m + 1) * 128], hT[:, k, :]) for k in range(8)], tw, ht, bk.free)
                    toks[m] = rows(bk, tok, m, dst[:, m, :], gain)
                b.free = [tok]
            b, w, tw = slab(t["win2"][2])
            vt = [None] * 4
            for m in range(4):
                bk = ring.next()
                tok = mm(bk.ap, [(hT[:, k, m * 128:(m + 1) * 128], w[:, k, :]) for k in range(8)], tw, ht, bk.free)
                vt[m] = act(vtok[:, m, :], bk.ap, ACT.Copy, tok, region_free)
                bk.free = [vt[m]]
            b.free = [tok]
            mods(2)

            ring_keep = ring
            ring = Ring(banks[0:6])
            its = [(h, i) for h in range(8) for i in range(4)]
            state = {}

            def att_a(n):
                h, i = its[n]
                L = 128 * (i + 1)
                o = 64 * (h % 2)
                bk = ring.next()
                q = mm(bk.ap[:, 0:L], [(qT[o:o + 64, h // 2, 128 * i:128 * i + 128], kT[o:o + 64, h // 2, 0:L])],
                       qt[h // 2], kt[h // 2], bk.free)
                sb = Sb[n % 3]
                s4 = sm[n % 4]
                t1 = stt(sb.ap[:, 0:L], bk.ap[:, 0:L], 0.125, T[:, h, 512 - L:512], ALU.mult, ALU.add,
                         q, t_T, sb.free)
                bk.free = [t1]
                t2 = red(s4.ap[:, 0:1], sb.ap[:, 0:L], ALU.max, t1, s4.free)
                t2 = ts(s4.ap[:, 1:2], s4.ap[:, 0:1], -1.0, ALU.mult, t2)
                t3 = act(sb.ap[:, 0:L], sb.ap[:, 0:L], ACT.Exp, t2, bias=s4.ap[:, 1:2], accum=s4.ap[:, 2:3])
                state[n] = t3

            def att_b(n):
                h, i = its[n]
                L = 128 * (i + 1)
                sb = Sb[n % 3]
                s4 = sm[n % 4]
                t3 = state.pop(n)
                t4 = recip(s4.ap[:, 3:4], s4.ap[:, 2:3], t3)
                t5 = ts(sb.ap[:, 0:L], sb.ap[:, 0:L], s4.ap[:, 3:4], ALU.mult, t4)
                s4.free = [t5]
                bk = ring.next()
                for j in range(i + 1):
                    q = tr(bk.ap[:, 128 * j:128 * j + 128], sb.ap[:, 128 * j:128 * j + 128], 128, t5, bk.free)
                sb.free = [q]
                pt = PT[h % 2]
                t6 = act(pt.ap[:, 0:i + 1, 128 * i:128 * i + 128], bk.ap[:, 0:L].rearrange("p (j n) -> p j n", n=128),
                         ACT.Copy, q, pt.free if i == 0 else None)
                bk.free = [t6]
                if i == 3:
                    o = 64 * (h % 2)
                    bo = banks[6 + h // 2 % 2]
                    for j in range(4):
                        q = mm(bo.ap[o:o + 64, 128 * j:512], [(vtok[:, j, 64 * h:64 * h + 64], pt.ap[:, j, 128 * j:512])],
                               t6, vt[j], bo.free, start=j == 0, stop=j == 3)
                    pt.free = [q]
                    if h % 2:
                        att_tok[h // 2] = act(mix[:, h // 2, :], bo.ap, ACT.Copy, q)
                        bo.free = [att_tok[h // 2]]

            att_tok = [None] * 4
            for n in range(len(its) + 1):
                if n < len(its):
                    att_a(n)
                if n:
                    att_b(n - 1)
            ring = ring_keep
            bk = ring.next()
            for k in range(4):
                _, tok = sq_stat(bk, mix[:, k, :], k, 4, ones, att_tok[k])
            r, ra, tr_ = rstd(bk, tok, 512)
            mt = [None] * 8
            for k in range(4):
                mt[k] = stt(mix[:, k, :], mix[:, k, :], cc("aog", k), ra, ALU.mult, ALU.mult, tr_, att_tok[k])
            r.free = [mt[3]]
            aft = [mt[3]]
            mods(2)

            at[0] = mark
            Q = take(2048).rearrange("p (k n) -> p k n", k=4)
            K = take(2048).rearrange("p (k n) -> p k n", k=4)
            V = take(2048).rearrange("p (k n) -> p k n", k=4)
            GB = take(2048).rearrange("p (k n) -> p k n", k=4)
            Vtk = take(2048).rearrange("p (c n) -> p c n", c=4)
            Ktk = take(2048).rearrange("p (c n) -> p c n", c=4)
            bT = take(512)[0:4, :]
            gT = take(512)[0:4, :]
            btok = take(16).rearrange("p (c h) -> p c h", c=4)
            gtok = take(16).rearrange("p (c h) -> p c h", c=4)
            eg = take(16).rearrange("p (c h) -> p c h", c=4)
            eb = take(16).rearrange("p (c h) -> p c h", c=4)
            wk = take(16).rearrange("p (c h) -> p c h", c=4)
            gl = take(16).rearrange("p (c h) -> p c h", c=4)
            nega = take(1)
            Lt = Bank(take(512))
            At = [Bank(take(512)) for _ in range(2)]
            Xb = Bank(take(512))
            Db = Bank(take(512))
            DTb = [Bank(take(512)) for _ in range(2)]
            dcy = Bank(take(512))
            Sst = Bank(take(512))
            Rb = Bank(take(512))
            Vn = Bank(take(512))
            v4 = lambda a: a.rearrange("p (h n) -> p h n", h=4)
            fl = lambda a: a.rearrange("p c h -> p (c h)")
            bc = lambda a, n=128: a.unsqueeze(2).broadcast_to([128, 4, n])

            b, w, tw = slab(t["win2ba"], 8, 8)
            bkb, bka = ring.next(), ring.next()
            tb = mm(bkb.ap[0:4, :], [(w[:, k, 0:4], hT[:, k, :]) for k in range(8)], tw, ht, bkb.free)
            ta = mm(bka.ap[0:4, :], [(w[:, k, 4:8], hT[:, k, :]) for k in range(8)], bka.free)
            b.free = [ta]
            t_b = act(bT, bkb.ap[0:4, :], ACT.Sigmoid, tb, aft)
            bkb.free = [t_b]
            t1 = act(gT, bka.ap[0:4, :], ACT.Identity, ta, aft, bias=cc("ddt")[0:4, :])
            bka.free = [t1]
            tn = act(nega[0:4, :], cc("dal")[0:4, :], ACT.Exp, aft)
            tn = ts(nega[0:4, :], nega[0:4, :], -1.0, ALU.mult, tn)
            sp3 = [tmp.next() for _ in range(3)]
            t2 = softplus(gT, [s.ap[0:4, :] for s in sp3], t1, *[s.free for s in sp3])
            for s in sp3:
                s.free = [t2]
            t3 = ts(gT, gT, nega[0:4, 0:1], ALU.mult, t2, tn)
            bk = ring.next()
            for c in range(4):
                q = tr(bk.ap[:, 4 * c:4 * c + 4], bT[:, 128 * c:128 * c + 128], 4, t_b, bk.free)
                q = tr(bk.ap[:, 16 + 4 * c:20 + 4 * c], gT[:, 128 * c:128 * c + 128], 4, t3)
            e1 = act(fl(btok), bk.ap[:, 0:16], ACT.Copy, q, aft)
            e2 = act(fl(gtok), bk.ap[:, 16:32], ACT.Copy, q, aft)
            bk.free = [e1, e2]
            bk = ring.next()
            q = mm(bk.ap[:, 0:16], [(tri, fl(gtok))], e2, bk.free)
            q2 = mm(bk.ap[:, 16:32], [(ones, fl(gtok))])
            q2 = mm(bk.ap[:, 32:48], [(gt_, fl(gtok))])
            e4 = act(fl(eg), bk.ap[:, 0:16], ACT.Exp, q2, aft)
            e6 = act(fl(wk), bk.ap[:, 32:48], ACT.Exp, aft)
            e7 = act(fl(gl), bk.ap[:, 16:32], ACT.Exp, aft)
            e5 = tt(fl(eb), fl(eg), fl(btok), ALU.mult, e4, e1, aft)
            bk.free = [e7]

            qk = {}
            for j, dst in enumerate((Q, K, V)):
                b, w, tw = slab(t["win2"][3 + j])
                for m in range(4):
                    bk = ring.next()
                    tok = mm(bk.ap, [(w[:, k, m * 128:(m + 1) * 128], hT[:, k, :]) for k in range(8)], tw, ht, bk.free)
                    t1 = conv4(bk, dst[:, m, :], COL["dcw"], 4 * j + m, 12, tok, aft)
                    if j < 2:
                        bk2 = ring.next()
                        _, tq = sq_stat(bk2, dst[:, m, :], 0, 1, ones, t1)
                        r, ra, tr_ = rstd(bk2, tq, 1.0)
                        t1 = stt(dst[:, m, :], dst[:, m, :], 128.0 ** -0.5 if j == 0 else 1.0, ra, ALU.mult, ALU.mult, tr_, t1)
                        r.free = [t1]
                    qk[j, m] = t1
                b.free = [tok]
            for c in range(4):
                cs = slice(128 * c, 128 * c + 128)
                bk, bk2 = ring.next(), ring.next()
                for h in range(4):
                    q = tr(bk.ap[:, 128 * h:128 * h + 128], K[:, h, cs], 128, qk[1, h], bk.free)
                    q2 = tr(bk2.ap[:, 128 * h:128 * h + 128], V[:, h, cs], 128, qk[2, h], bk2.free)
                qk["k", c] = tt(v4(Ktk[:, c, :]), v4(bk.ap), bc(wk[:, c, :]), ALU.mult, q, e6, aft)
                qk["v", c] = tt(v4(Vtk[:, c, :]), v4(bk2.ap), bc(btok[:, c, :]), ALU.mult, q2, e1, aft)
                bk.free, bk2.free = [qk["k", c]], [qk["v", c]]
            vfree = [q2]
            for h in range(4):
                bk = ring.next()
                for c in range(4):
                    q = mm(bk.ap[:, 128 * c:128 * c + 128], [(btok[:, c, h:h + 1].broadcast_to([128, 128]), ident)],
                           e1, bk.free)
                qk["kb", h] = tt(V[:, h, :], bk.ap, K[:, h, :], ALU.mult, q, qk[1, h], vfree)
                bk.free = [qk["kb", h]]

            for c in range(4):
                cs = slice(128 * c, 128 * c + 128)
                A_ = At[c % 2]
                tm = tt(v4(dcy.ap), gt_.unsqueeze(1).broadcast_to([128, 4, 128]), bc(gtok[:, c, :]), ALU.mult,
                        e2, t_const, dcy.free, aft)
                bk = ring.next()
                for h in range(4):
                    hs = slice(128 * h, 128 * h + 128)
                    q = mm(bk.ap[:, hs], [(dcy.ap[:, hs], tri)], tm, bk.free)
                t1 = act(dcy.ap, bk.ap, ACT.Exp, q)
                bk.free = [t1]
                if c:
                    bk = ring.next()
                    for h in range(4):
                        q = mm(bk.ap[:, 128 * h:128 * h + 128], [(gtok[:, c, h:h + 1].broadcast_to([128, 128]), tri)],
                               bk.free)
                    tE = act(GB[:, :, cs], v4(bk.ap), ACT.Exp, q, aft)
                    bk.free = [tE]
                    tE = tt(GB[:, :, cs], GB[:, :, cs], Q[:, :, cs], ALU.mult, tE, [qk[0, h] for h in range(4)])
                else:
                    tE = None
                t1 = tt(v4(dcy.ap), v4(dcy.ap), tri.unsqueeze(1).broadcast_to([128, 4, 128]), ALU.mult, t1)
                bk, bk2 = ring.next(), ring.next()
                for h in range(4):
                    hs = slice(128 * h, 128 * h + 128)
                    q = mm(bk.ap[:, hs], [(K[:, h, cs], V[:, h, cs])], qk["kb", h], bk.free)
                    q2 = mm(bk2.ap[:, hs], [(K[:, h, cs], Q[:, h, cs])], qk[0, h], bk2.free)
                tA = tt(A_.ap, bk2.ap, dcy.ap, ALU.mult, q2, t1, A_.free, aft)
                tL = tt(Lt.ap, bk.ap, dcy.ap, ALU.mult, q, t1, Lt.free, aft)
                bk.free, bk2.free = [tL], [tA]
                dcy.free = [tL]
                tL = tt(v4(Lt.ap), v4(Lt.ap), tris.unsqueeze(1).broadcast_to([128, 4, 128]), ALU.mult, tL)
                DT = DTb[c % 2]
                bk = ring.next()
                for h in range(4):
                    hs = slice(128 * h, 128 * h + 128)
                    q = tr(bk.ap[:, hs], Lt.ap[:, hs], 128, tL, bk.free)
                tX = tt(v4(Xb.ap), v4(bk.ap), const[:, CLEV, :].unsqueeze(1).broadcast_to([128, 4, 128]), ALU.mult,
                        q, Xb.free, aft)
                bk.free = [tX]
                idb = ident.unsqueeze(1).broadcast_to([128, 4, 128])
                tD = tt(v4(Db.ap), idb, v4(Xb.ap), ALU.subtract, tX, Db.free, aft)
                bk = ring.next()
                for h in range(4):
                    hs = slice(128 * h, 128 * h + 128)
                    q = mm(bk.ap[:, hs], [(Xb.ap[:, hs], ident)], tX, bk.free)
                tDT = stt(v4(DT.ap), v4(bk.ap), -1.0, idb, ALU.mult, ALU.add, q, DT.free, aft)
                bk.free = [tDT]
                Xb.free = [q, tD]
                for lev in range(1, 7):
                    last = lev == 6
                    bk = ring.next()
                    for h in range(4):
                        hs = slice(128 * h, 128 * h + 128)
                        q = mm(bk.ap[:, hs], [(Lt.ap[:, hs], Db.ap[:, hs])], tL, tD, bk.free)
                    tX = tt(v4(Xb.ap), v4(bk.ap), const[:, CLEV + lev, :].unsqueeze(1).broadcast_to([128, 4, 128]),
                            ALU.mult, q, Xb.free)
                    bk.free = [tX]
                    if last:
                        Lt.free = [q]
                        Db.free = [q]
                    bk, bk2 = ring.next(), ring.next()
                    for h in range(4):
                        hs = slice(128 * h, 128 * h + 128)
                        q2 = mm(bk2.ap[:, hs], [(Xb.ap[:, hs], DT.ap[:, hs])], tX, tDT, bk2.free)
                    if not last:
                        for h in range(4):
                            hs = slice(128 * h, 128 * h + 128)
                            q1 = mm(bk.ap[:, hs], [(DT.ap[:, hs], Xb.ap[:, hs])], tX, tDT, bk.free)
                        tD = tt(Db.ap, Db.ap, bk.ap, ALU.subtract, q1, tD)
                        bk.free = [tD]
                        Xb.free = [q1, q2]
                        tDT = tt(DT.ap, DT.ap, bk2.ap, ALU.subtract, q2, q1)
                    else:
                        Xb.free = [q2]
                        tDT = tt(DT.ap, DT.ap, bk2.ap, ALU.subtract, q2)
                    bk2.free = [tDT]
                if c:
                    bk = ring.next()
                    for h in range(4):
                        hs = slice(128 * h, 128 * h + 128)
                        q = mm(bk.ap[:, hs], [(K[:, h, cs], Sst.ap[:, hs])], Sst.tok, bk.free)
                    t1 = tt(v4(Rb.ap), v4(bk.ap), bc(eb[:, c, :]), ALU.mult, q, e5, Rb.free)
                    bk.free = [t1]
                    tR = tt(Rb.ap, Vtk[:, c, :], Rb.ap, ALU.subtract, t1, qk["v", c])
                    rsrc = Rb.ap
                else:
                    tR = qk["v", 0]
                    rsrc = Vtk[:, 0, :]
                bk = ring.next()
                for h in range(4):
                    hs = slice(128 * h, 128 * h + 128)
                    q = mm(bk.ap[:, hs], [(DT.ap[:, hs], rsrc[:, hs])], tDT, tR, bk.free)
                Rb.free = [q]
                DT.free = [q]
                tV = act(Vn.ap, bk.ap, ACT.Copy, q, Vn.free, aft)
                bk.free = [tV]
                bk = ring.next()
                for h in range(4):
                    hs = slice(128 * h, 128 * h + 128)
                    pairs = [(Vn.ap[:, hs], A_.ap[:, hs])]
                    if c:
                        pairs.append((Sst.ap[:, hs], GB[:, h, cs]))
                    q = mm(bk.ap[:, hs], pairs, tV, tA, tE, bk.free)
                A_.free = [q]
                o_tok = act(mix[:, 4:8, cs], v4(bk.ap), ACT.Copy, q)
                bk.free = [o_tok]
                mt[4 + c] = o_tok
                if c < 3:
                    bk = ring.next()
                    for h in range(4):
                        hs = slice(128 * h, 128 * h + 128)
                        q3 = mm(bk.ap[:, hs], [(Ktk[:, c, hs], Vn.ap[:, hs])], qk["k", c], bk.free)
                    if c == 0:
                        Sst.tok = act(Sst.ap, bk.ap, ACT.Copy, q3, aft)
                    else:
                        t1 = tt(v4(Sst.ap), v4(Sst.ap), bc(gl[:, c, :]), ALU.mult, e7, Sst.tok, q)
                        Sst.tok = tt(Sst.ap, bk.ap, Sst.ap, ALU.add, q3, t1)
                    bk.free = [Sst.tok]
                    Vn.free = [q3]
                else:
                    Vn.free = [q]
            ot = mt[4:8]
            b, w, tw = slab(t["win2"][6])
            for m in range(4):
                bk = ring.next()
                tok = mm(bk.ap, [(w[:, k, m * 128:(m + 1) * 128], hT[:, k, :]) for k in range(8)], tw, ht, bk.free)
                sb = tmp.next()
                tz = act(sb.ap, bk.ap, ACT.Silu, tok, sb.free)
                bk.free = [tz]
                bk2 = ring.next()
                _, tq = sq_stat(bk2, mix[:, 4 + m, :], 0, 1, ones, ot)
                r, ra, tr_ = rstd(bk2, tq, 128)
                t1 = stt(mix[:, 4 + m, :], mix[:, 4 + m, :], cc("dog"), ra, ALU.mult, ALU.mult, tr_, ot)
                r.free = [t1]
                mt[4 + m] = tt(mix[:, 4 + m, :], mix[:, 4 + m, :], sb.ap, ALU.mult, t1, tz)
                sb.free = [mt[4 + m]]
            b.free = [tok]
            mods(3)
            out_proj([[(t["wout2"][g], 0, 8)] for g in range(2)], lambda k: mix[:, k, :], mt, None, None, False, 4, t_post)
            for k in range(8):
                h_free[k] = [tok]
            region_free[:] = list(xtok[7])

        def peer():
            nonlocal ring
            t_pre, t_post = derived(5)
            ht = pre_norm(5, t_pre)
            at[0] = BASE
            qry = take(16 * 512).rearrange("p (k n) -> p k n", k=16)
            slots_at = at[0]
            qt = [None] * 16
            for j in range(4):
                b, w, tw = slab(t["pq"][j])
                for m in range(4):
                    kk = 4 * j + m
                    bk = ring.next()
                    tok = mm(bk.ap, [(w[:, k, m * 128:(m + 1) * 128], hT[:, k, :]) for k in range(8)], tw, ht, bk.free)
                    qt[kk] = act(qry[:, kk, :], bk.ap, ACT.Copy, tok, region_free)
                    if m % 2 == 0:
                        bk2 = ring.next()
                    _, tq = sq_stat(bk2, bk.ap, m % 2, 2, ones, tok)
                    bk.free = [qt[kk], (P.sem["act"], P.n["act"])]
                    if m % 2:
                        r, ra, tr_ = rstd(bk2, tq, 256)
                        for u in (1, 0):
                            i = kk - u
                            qt[i] = stt(qry[:, i, :], qry[:, i, :], cc("pqg", 1 - u), ra, ALU.mult, ALU.mult, tr_, qt[i])
                        r.free = [qt[kk]]
                b.free = [tok]
            done = [tok]
            slab_free = [x for s in slabs.banks for x in s.free]
            keys = slabs.banks[0].ap[:, 0:256].rearrange("p (a n) -> p a n", a=2)
            tkeys = P.dma("sp", slabs.banks[0].ap[:, 0:256], t["keys"], slabs.banks[0].free, slot=slabs.banks[0])
            tiota = P.dma("sp", slabs.banks[0].ap[:, 256:272], t["iota"], slabs.banks[0].free)
            iota = slabs.banks[0].ap[:, 256:272]

            o = 272
            base0 = slabs.banks[0].ap
            gB = base0[:, 512:1536]
            Sc = base0[:, 1536:3584].rearrange("p (a n) -> p a n", a=16)
            small = base0[:, 3584:4096]
            htk = slabs.banks[1].ap.rearrange("p (c n) -> p c n", c=4)
            cand = slabs.banks[2].ap[:, 0:2048].rearrange("p (h n) -> p h n", h=8)
            eq = slabs.banks[2].ap[:, 2048:4096]
            f1, f2 = slabs.banks[1].free, slabs.banks[2].free
            tht = [None] * 4
            for c in range(4):
                for k in range(8):
                    if k % 4 == 0:
                        bk = ring.next()
                    q = tr(bk.ap[:, 128 * (k % 4):128 * (k % 4) + 128], hT[:, k, 128 * c:128 * c + 128], 128, ht[k], bk.free)
                    if k % 4 == 3:
                        tht[c] = act(htk[:, c, 512 * (k // 4):512 * (k // 4) + 512], bk.ap, ACT.Copy, q, f1)
                        bk.free = [tht[c]]
            hfree = [q]
            for k in range(8):
                if k % 4 == 0:
                    bk = ring.next()
                q = mm(bk.ap[:, 128 * (k % 4):128 * (k % 4) + 128], [(post(5, k).broadcast_to([128, 128]), ident)],
                       t_post, bk.free)
                if k % 4 == 3:
                    tgB = act(gB[:, 512 * (k // 4):512 * (k // 4) + 512], bk.ap, ACT.Copy, q, slabs.banks[0].free)
                    bk.free = [tgB]
            xtk = hT.rearrange("p k n -> p (k n)").rearrange("p (c n) -> p c n", c=4)
            txt = [None] * 4
            for c in range(4):
                for k in range(8):
                    if k % 4 == 0:
                        bk = ring.next()
                    q = tr(bk.ap[:, 128 * (k % 4):128 * (k % 4) + 128], xT[:, k, 128 * c:128 * c + 128], 128, xtok[k], bk.free)
                    if k % 4 == 3:
                        txt[c] = act(xtk[:, c, 512 * (k // 4):512 * (k // 4) + 512], bk.ap, ACT.Copy, q, hfree, done)
                        bk.free = [txt[c]]
            xfree = [q]

            ringmem = [take(2048) for _ in range((53000 - at[0]) // 2048 - 1)]
            xflat = xT.rearrange("p k n -> p (k n)")
            gslots = [Bank(m, P.new_sem()) for m in ringmem]
            for g in gslots:
                g.free = list(region_free) + done
            for m in (xflat[:, 0:2048], xflat[:, 2048:4096]):
                g = Bank(m, P.new_sem())
                g.free = list(xfree)
                gslots.append(g)
            NG = len(gslots)
            sm_at = [0]

            def smt(n, src=small):
                a = sm_at[0]
                sm_at[0] += n
                assert sm_at[0] <= 512
                return src[:, a:a + n]
            vals = smt(256).rearrange("p (a n) -> p a n", a=16)
            big = take(1900)
            bat = [0]

            def bg(n):
                a = bat[0]
                bat[0] += n
                assert bat[0] <= 1900
                return big[:, a:a + n]
            vidx = bg(256).bitcast(U32).rearrange("p (a n) -> p a n", a=16)
            vif = bg(256).rearrange("p (a n) -> p a n", a=16)
            tv = bg(128).rearrange("p (h n) -> p h n", h=8)
            tpos = bg(128).bitcast(U32).rearrange("p (h n) -> p h n", h=8)
            tab = bg(128).bitcast(U32)
            taf = bg(128)
            ea = bg(128)
            sm8 = bg(16)
            gates = [bg(128) for _ in range(2)]
            eidx = [bg(128).bitcast(U32) for _ in range(2)]
            dots = [Bank(bg(GG)) for _ in range(4)]
            diag = [Bank(tmp.banks[i].ap[:, 128 * j:128 * j + 128]) for i in range(4, 8) for j in range(2)]
            for i, dgb in enumerate(diag):
                dgb.free = list(tmp.banks[4 + i // 2].free)
            gate_free = [[], []]
            idx_free = [[], []]
            tmpfree = [x for i in range(8) for x in tmp.banks[i].free]
            rank = Ring(banks[4:8])
            ready = {}
            prevt = [tmpfree + list(region_free) + done + f2 + [tkeys, tiota]]

            def topk(c):
                cs = slice(128 * c, 128 * c + 128)
                sct = []
                for k4 in range(4):
                    bk = rank.next()
                    for i in range(4):
                        kk = 4 * k4 + i
                        q = mm(bk.ap[:, 128 * i:128 * i + 128], [(qry[:, kk, cs], keys[:, kk % 2, :])],
                               qt[kk], tkeys, bk.free)
                    tS = act(Sc[:, 4 * k4:4 * k4 + 4, :], bk.ap.rearrange("p (a n) -> p a n", a=4), ACT.Copy, q, prevt[0])
                    bk.free = [tS]
                    sct.append(tS)
                yield
                last = None
                for a in range(16):
                    s_ = Sc[:, a, :]
                    t1 = vmax(vals[:, a, 0:8], s_, sct[a // 4], prevt[0])
                    t2 = vindex(vidx[:, a, 0:8], vals[:, a, 0:8], s_, t1)
                    t3 = vdrop(s_, vals[:, a, 0:8], s_, t2)
                    t4 = vmax(vals[:, a, 8:16], s_, t3)
                    last = vindex(vidx[:, a, 8:16], vals[:, a, 8:16], s_, t4)
                    yield
                fi = vcopy(vif.rearrange("p a n -> p (a n)"), vidx.rearrange("p a n -> p (a n)"), last)
                va = vals.rearrange("p (h two) n -> p h two n", two=2)
                ia = vif.rearrange("p (h two) n -> p h two n", two=2)
                c4 = cand.rearrange("p h (a b) -> p h a b", a=16)
                t1 = tt(c4, va[:, :, 0, :].unsqueeze(3).broadcast_to([128, 8, 16, 16]),
                        va[:, :, 1, :].unsqueeze(2).broadcast_to([128, 8, 16, 16]), ALU.add, last)
                yield
                for h in range(8):
                    s_ = cand[:, h, :]
                    t2 = vmax(tv[:, h, 0:8], s_, t1)
                    t3 = vindex(tpos[:, h, 0:8], tv[:, h, 0:8], s_, t2)
                    t4 = vdrop(s_, tv[:, h, 0:8], s_, t3)
                    t5 = vmax(tv[:, h, 8:16], s_, t4)
                    last = vindex(tpos[:, h, 8:16], tv[:, h, 8:16], s_, t5)
                    yield
                posf = tpos.rearrange("p h n -> p (h n)")
                e4 = eq.rearrange("p (h k a) -> p h k a", h=8, k=16)
                iob = iota.unsqueeze(1).broadcast_to([128, 128, 16])
                t6 = fi
                for u in range(2):
                    if u == 0:
                        t1 = ts(tab, posf, 4, ALU.logical_shift_right, last)
                    else:
                        t1 = ts(tab, posf, 15, ALU.bitwise_and, t2)
                    t2 = vcopy(taf, tab, t1, t6)
                    t3 = tt(eq.rearrange("p (k a) -> p k a", a=16), taf.unsqueeze(2).broadcast_to([128, 128, 16]), iob,
                            ALU.is_equal, t2, t6)
                    yield
                    t4 = tt(e4, e4, ia[:, :, u, :].unsqueeze(2).broadcast_to([128, 8, 16, 16]), ALU.mult, t3, fi)
                    yield
                    dst = ea if u == 0 else taf
                    t6 = red(dst, eq.rearrange("p (k a) -> p k a", a=16), ALU.add, t4)
                    yield
                t7 = stt(ea, ea, 128.0, taf, ALU.mult, ALU.add, t6)
                t8 = vcopy(eidx[c % 2], ea, t7, idx_free[c % 2])
                tvb = tv[:, :, 0:1].broadcast_to([128, 8, 16])
                g3 = gates[c % 2].rearrange("p (h n) -> p h n", h=8)
                g1 = tt(g3, tv, tvb, ALU.subtract, last, gate_free[c % 2])
                g2 = act(gates[c % 2], gates[c % 2], ACT.Exp, g1)
                g4 = red(sm8[:, 0:8], g3, ALU.add, g2)
                g5 = recip(sm8[:, 8:16], sm8[:, 0:8], g4)
                g6 = tt(g3, g3, sm8[:, 8:16].unsqueeze(2).broadcast_to([128, 8, 16]), ALU.mult, g5)
                prevt[0] = [t8, g6]
                ready[c] = (t8, g6)
                yield

            for _ in topk(0):
                pass
            tv_ = t["experts"]
            n = 0
            gfin = [Bank(m) for m in (tmp.banks[0].ap, tmp.banks[1].ap, tmp.banks[2].ap, tmp.banks[3].ap)]
            for i, g in enumerate(gfin):
                g.free = list(tmp.banks[i].free)
            for c in range(4):
                tidx, tgate = ready[c]
                nxt = topk(c + 1) if c < 3 else iter(())
                acc = [banks[2 * (c % 2)], banks[2 * (c % 2) + 1]]
                for grp in range(128 // GG):
                    sl = []
                    for i in range(GG):
                        s_i = grp * GG + i
                        gs = gslots[n % NG]
                        n += 1
                        gs.uses += 1
                        P.q["pool"].append((
                            lambda e, gs=gs, s_i=s_i, c=c: e.indirect_dma_start(
                                out=gs.ap, out_offset=None, in_=tv_,
                                in_offset=bass.IndirectOffsetOnAxis(ap=eidx[c % 2][:, s_i:s_i + 1], axis=0)),
                            [tidx] + gs.free, gs.sem, 16))
                        tg = (gs.sem, 16 * gs.uses)
                        dt_ = dots[grp % 4]
                        t1 = put("dve", lambda e, gs=gs, i=i, dt_=dt_, c=c: e.tensor_tensor_reduce(
                            gs.ap[:, 0:1024], gs.ap[:, 0:1024], htk[:, c, :], 1.0, 0.0, ALU.mult, ALU.add,
                            dt_.ap[:, i:i + 1]), tg, tht[c], dt_.free if i == 0 else None)
                        sl.append((gs, tg, t1))
                    dt_ = dots[grp % 4]
                    t2 = act(dt_.ap, dt_.ap, ACT.Gelu, t1)
                    t3 = tt(dt_.ap, dt_.ap, gates[c % 2][:, grp * GG:grp * GG + GG], ALU.mult, t2, tgate)
                    for i in range(GG):
                        s_i = grp * GG + i
                        gs, tg, t1 = sl[i]
                        dg = diag[(grp * GG + i) % 8]
                        t4 = act(dg.ap, ident, ACT.Copy, t3, dg.free, scale=dt_.ap[:, i:i + 1])
                        for u in range(2):
                            q = mm(acc[u].ap, [(dg.ap, gs.ap[:, 1024 + 512 * u:1536 + 512 * u])], t4, tg,
                                   acc[u].free if s_i == 0 else None, start=s_i == 0, stop=s_i == 127)
                        dg.free = [q]
                        gs.free = [q, t1]
                    dt_.free = [t4]
                    next(nxt, None)
                    next(nxt, None)
                idx_free[c % 2] = [gs.free[0]]
                gate_free[c % 2] = [t3]
                for _ in nxt:
                    pass
                for u in range(2):
                    f = gfin[2 * (c % 2) + u]
                    us = slice(512 * u, 512 * u + 512)
                    t5 = tt(f.ap, acc[u].ap, gB[:, us], ALU.mult, q, tgB, f.free)
                    acc[u].free = [t5]
                    t6 = tt(f.ap, f.ap, xtk[:, c, us], ALU.add, t5, txt[c])
                    tk = P.dma("sp", out[0, 128 * c:128 * c + 128, us], f.ap, t6, store=True)
                    f.free = [tk]

        phases = [conv_mixer, lambda: ffn(0, 1), ssd_mixer, lambda: ffn(1, 3), hybrid, peer]
        for ph in phases:
            ph()

        block = ctx.enter_context(nc.Block())

        @block.sync
        def _(e):
            P.replay("sp", e)
            for s, v in P.stores:
                e.wait_ge(s, v)

        @block.gpsimd
        def _(e):
            P.replay("pool", e)

        @block.scalar
        def _(e):
            P.replay("act", e)

        @block.tensor
        def _(e):
            P.replay("pe", e)

        @block.vector
        def _(e):
            P.replay("dve", e)


def _layout(inputs):
    import numpy as np

    g = {k: np.asarray(v) for k, v in inputs.items()}

    def slabs(w, width=512):
        k, n = w.shape
        return np.ascontiguousarray(
            w.reshape(k // 128, 128, n // width, width).transpose(2, 1, 0, 3).reshape(n // width, 128, -1))

    def colv(v):
        return v.reshape(-1, 128).T

    a = {}
    a["xT"] = np.ascontiguousarray(g["x"][0].reshape(S, 8, 128).transpose(2, 1, 0).reshape(128, -1))
    a["ada"] = slabs(g["ada_w"])
    a["ada2"] = slabs(g["w_ada_2"][0])
    w = g["a_w_in"][0]
    a["ain"] = slabs(np.concatenate([w[:, 1024:2048], w[:, 2048:3072], w[:, 0:1024]], axis=1))
    a["aout"] = slabs(g["a_w_out"][0])
    w = g["m_w_in"][0]
    a["mdt"] = slabs(w[:, 6144:6176], 32)[0]
    a["mxbc"] = slabs(np.concatenate([w[:, 4096:5120], w[:, 5120:6144], w[:, 2048:4096]], axis=1))
    a["mz"] = slabs(w[:, 0:2048])
    a["mout"] = slabs(g["m_w_out"][0])
    fi = []
    fo = []
    for i in range(2):
        w = g["f_w_in"][i]
        w = np.concatenate([w[:, 0:FF].reshape(D, 11, 256), w[:, FF:2 * FF].reshape(D, 11, 256)], axis=2)
        fi.append(slabs(w.reshape(D, 2 * FF)))
        fo.append(slabs(g["f_w_out"][i]))
    a["fin"] = np.stack(fi)
    a["fout"] = np.stack(fo)
    w = g["w_in_2"][0]
    a["win2"] = slabs(w[:, 0:3584])
    a["win2ba"] = slabs(w[:, 3584:3592], 8)[0]
    a["wout2"] = slabs(g["w_out_2"][0])
    a["pq"] = slabs(g["peer_w_query_2"][0])
    a["keys"] = np.ascontiguousarray(np.concatenate(
        [g["peer_sub_keys_1_2"][0].T, g["peer_sub_keys_2_2"][0].T], axis=1))
    a["iota"] = np.ascontiguousarray(np.broadcast_to(np.arange(16, dtype=np.float32), (128, 16)))
    a["experts"] = np.concatenate([g["peer_expert_down_2"][0], g["peer_expert_up_2"][0]], axis=1)
    d = 384 + np.arange(128)[:, None] - np.arange(512)[None, :]
    idx = np.clip(d, -128, 128) + 128
    a["relT"] = np.ascontiguousarray(g["attn_rel_bias_2"][0][:, idx].transpose(1, 0, 2).reshape(128, -1))

    col = np.zeros((128, NCOL), np.float32)

    def place(name, v):
        v = v if v.ndim == 2 else v[:, None]
        col[:v.shape[0], COL[name]:COL[name] + v.shape[1]] = v

    place("c", colv(g["c"][0]))
    place("adab", colv(g["ada_b"]))
    place("ng", colv(g["norm_g"].reshape(-1)))
    place("acw", colv(g["a_conv_w"][0].reshape(-1)))
    place("mcw", colv(g["m_conv_w"][0].reshape(-1)))
    place("mcb", colv(g["m_conv_b"][0]))
    place("mng", colv(g["m_norm_g"][0]))
    place("md", colv(np.repeat(g["m_d"][0], 64)))
    place("c2", colv(g["c_2"][0]))
    place("adab2", colv(g["b_ada_2"][0]))
    place("n1", colv(g["norm1_gain_2"][0]))
    place("n2", colv(g["norm2_gain_2"][0]))
    place("aog", colv(g["attn_out_gain_2"][0]))
    place("qg", np.tile(g["attn_q_gain_2"][0], 2))
    place("kg", np.tile(g["attn_k_gain_2"][0], 2))
    place("dcw", colv(g["dn_conv_w_2"][0].reshape(-1)))
    place("dog", g["dn_out_gain_2"][0])
    place("pqg", colv(g["peer_query_gain_2"][0]))
    place("mdt", g["m_dt_bias"][0])
    place("mal", g["m_a_log"][0])
    place("dal", g["dn_a_log_2"][0])
    place("ddt", g["dn_dt_bias_2"][0])
    a["cols"] = col

    i, j = np.arange(128)[:, None], np.arange(128)[None, :]
    cs = [i == j, i <= j, i < j, i // 64 == j // 64, (i >= 0) & (j >= 0), i > j]
    for b in LEVELS:
        cs.append((i // (2 * b) == j // (2 * b)) & ((i // b) % 2 == 1) & ((j // b) % 2 == 0))
    a["consts"] = np.ascontiguousarray(np.stack([np.broadcast_to(m, (128, 128)) for m in cs], 1)
                                       .reshape(128, -1).astype(np.float32))
    return a


def kernel(**inputs):
    import numpy as _np
    import concourse.bacc as _bacc
    from concourse import mybir as _mybir
    from concourse.bass_utils import run_bass_kernel_spmd as _run

    nc = _bacc.Bacc("TRN2", target_bir_lowering=False, num_devices=1)
    arrays = {"in_" + k: v for k, v in _layout(inputs).items()}
    aps = {k: nc.dram_tensor("in_" + k, arrays["in_" + k].shape, _mybir.dt.float32, kind="ExternalInput").ap()
           for k in (n[3:] for n in arrays)}
    out = nc.dram_tensor("out", (1, S, D), _mybir.dt.float32, kind="ExternalOutput").ap()
    build(nc, aps, out)
    r = _run(nc, [arrays], core_ids=[0])
    return r.results[0]["out"]
```

```python
from contextlib import ExitStack

import concourse.bass as bass
from concourse import mybir

ALU = mybir.AluOpType
ACT = mybir.ActivationFunctionType
F32 = mybir.dt.float32
F32R = mybir.dt.float32r
U32 = mybir.dt.uint32
I32 = mybir.dt.int32
AX_X = mybir.AxisListType.X

D = 1024
S = 512
KD = 8
FF = 2816
KF = 22
EPS = 1e-6
WORDS = 53200
LOW = 15944
BASE = LOW + 8192 + 6144
GG = 2

_COLS = [("c", 8), ("adab", 96), ("ng", 64), ("acw", 24), ("mcw", 128), ("mcb", 32), ("mng", 16),
         ("md", 16), ("c2", 8), ("adab2", 48), ("n1", 8), ("n2", 8), ("aog", 4), ("qg", 1), ("kg", 1),
         ("dcw", 48), ("dog", 1), ("pqg", 2), ("mdt", 1), ("mal", 1), ("dal", 1), ("ddt", 1)]
COL = {}
_at = 0
for _n, _k in _COLS:
    COL[_n] = _at
    _at += _k
NCOL = _at
LEVELS = [1, 2, 4, 8, 16, 32, 64]
CIDENT, CTRI, CTRIS, CBLK, CONES, CGT = 0, 1, 2, 3, 4, 5
NCONST = 6


class Bank:

    def __init__(self, ap, sem=None):
        self.ap = ap
        self.sem = sem
        self.uses = 0
        self.free = []


class Ring:
    def __init__(self, banks):
        self.banks = banks
        self.n = 0

    def next(self):
        b = self.banks[self.n % len(self.banks)]
        self.n += 1
        return b


class Program:

    def __init__(self, nc, ctx):
        self.nc = nc
        self.ctx = ctx
        self.q = {e: [] for e in ("pe", "act", "dve", "pool", "sp")}
        self.sem = {e: ctx.enter_context(nc.semaphore("s_" + e)) for e in ("pe", "act", "dve", "pool")}
        self.n = {e: 0 for e in self.sem}
        self.nsem = 0
        self.stores = []

    def put(self, eng, fn, *waits, quiet=False):
        flat = []
        for w in waits:
            if w is None:
                continue
            flat.extend(w if isinstance(w, list) else [w])
        if quiet:
            self.q[eng].append((fn, flat, None, 0))
            return None
        self.n[eng] += 1
        self.q[eng].append((fn, flat, self.sem[eng], 1))
        return (self.sem[eng], self.n[eng])

    def new_sem(self):
        self.nsem += 1
        return self.ctx.enter_context(self.nc.semaphore(f"d{self.nsem}"))

    def dma(self, eng, out, in_, *waits, slot=None, store=False):
        if slot is None:
            slot = Bank(None, self.new_sem())
        slot.uses += 1
        flat = []
        for w in waits:
            if w is not None:
                flat.extend(w if isinstance(w, list) else [w])
        self.q[eng].append((lambda e: e.dma_start(out, in_), flat, slot.sem, 16))
        tok = (slot.sem, 16 * slot.uses)
        if store:
            self.stores.append(tok)
        return tok

    def replay(self, eng, e):
        seen = {}
        for fn, waits, sem, inc in self.q[eng]:
            need = {}
            for s, v in waits:
                need[s.name] = (s, max(v, need.get(s.name, (s, 0))[1]))
            for name, (s, v) in need.items():
                if seen.get(name, 0) < v:
                    e.wait_ge(s, v)
                    seen[name] = v
            ins = fn(e)
            if sem is not None:
                ins.then_inc(sem, inc)


def build(nc, t, out):
    ctx = ExitStack()
    with ctx:
        P = Program(nc, ctx)
        put = P.put

        base = (nc.sbuf_base + 31) // 32 * 32
        arena = ctx.enter_context(nc.sbuf_tensor("arena", [128, LOW], F32))
        psum = ctx.enter_context(nc.psum_tensor("psum", [128, 8, 512], F32))
        at = [0]

        def view(name, a, n, dt):
            return nc.alloc_sbuf_tensor_at(name, [128, n], dt, offset=base + 4 * a)[:, :]

        hf = view("h_f", LOW, 8192, F32)
        wf = view("w_f", LOW + 8192, 6144, F32)
        region = view("region", BASE, WORDS - BASE, F32)

        def take(n):
            a = at[0]
            at[0] += n
            assert at[0] <= WORDS, at[0]
            if a < LOW:
                assert at[0] <= LOW, at[0]
                return arena[:, a:a + n]
            return region[:, a - BASE:a - BASE + n]

        def take_r(n, a=None):
            if a is None:
                a = (at[0] + 7) // 8 * 8
                at[0] = a + n
                assert at[0] <= WORDS, at[0]
            views[0] += 1
            v = view(f"rounded{views[0]}", a, n, F32R)
            return v.bitcast(F32), v

        views = [0]
        const = take(NCONST * 128).rearrange("p (a n) -> p a n", n=128)
        col = take(NCOL)
        mod = take(144)
        der = take(160)
        csil = take(16)
        xT = take(4096).rearrange("p (k n) -> p k n", k=8)
        k8 = lambda a: a.rearrange("p (k n) -> p k n", k=8)
        raw_at = at[0]
        raw = Ring([Bank(take(1024), P.new_sem()) for _ in range(4)])
        tmp = Ring([Bank(take(512)) for _ in range(8)])
        macc = Ring([Bank(take(512)) for _ in range(2)])
        rst = Ring([Bank(take(512)) for _ in range(2)])
        assert LOW - at[0] < 8, (LOW, at[0])
        hhf, hhr = [k8(a) for a in take_r(4096, LOW)]
        hlf, hlr = [k8(a) for a in take_r(4096, LOW + 4096)]
        w_f, w_r = take_r(6144, LOW + 8192)
        whl = Ring([Bank((w_f[:, 2048 * i:2048 * i + 2048], w_r[:, 2048 * i:2048 * i + 2048])) for i in range(3)])

        banks = [Bank(psum[:, i, :]) for i in range(8)]
        ring = Ring(banks)

        def cc(name, i=0, n=1):
            a = COL[name] + i
            return col[:, a:a + n]

        ident = const[:, CIDENT, :]
        tri = const[:, CTRI, :]
        tris = const[:, CTRIS, :]
        blk = const[:, CBLK, :]
        ones = const[:, CONES, :]
        gt_ = const[:, CGT, :]

        def mm(o, pairs, *waits, start=True, stop=True, skip=False):
            n = len(pairs)
            for i, (a, b) in enumerate(pairs):
                def f(e, a=a, b=b, i=i):
                    return e.matmul(o, a, b, start=start and i == 0, stop=stop and i == n - 1,
                                    skip_group_check=skip)
                tok = put("pe", f, *(waits if i == 0 else ()), quiet=i < n - 1)
            return tok

        def tr(o, i_, p, *waits):
            return put("pe", lambda e: e.transpose(o, i_, ident[0:p, 0:p]), *waits)

        def act(o, i_, func, *waits, bias=0.0, scale=1.0, accum=None):
            def f(e):
                k = {} if accum is None else {"accum_out": accum}
                return e.activation(o, i_, func, bias=bias, scale=scale, **k)
            return put("act", f, *waits)

        def tt(o, a, b, op, *waits, eng="dve"):
            return put(eng, lambda e: e.tensor_tensor(o, a, b, op), *waits)

        def ts(o, a, s1, op0, *waits, s2=None, op1=None, eng="dve"):
            def f(e):
                if op1 is None:
                    return e.tensor_scalar(o, a, s1, None, op0)
                return e.tensor_scalar(o, a, s1, s2, op0, op1)
            return put(eng, f, *waits)

        def stt(o, a, s, b, op0, op1, *waits):
            return put("dve", lambda e: e.scalar_tensor_tensor(out=o, in0=a, scalar=s, in1=b, op0=op0, op1=op1),
                       *waits)

        def vmax(o, i_, *waits):
            return put("dve", lambda e: e.max(o, i_), *waits)

        def vindex(o, m, i_, *waits):
            return put("dve", lambda e: e.max_index(o, m, i_), *waits)

        def vdrop(o, m, i_, *waits):
            return put("dve", lambda e: e.match_replace(o, m, i_, -3.0e38), *waits)

        def vcopy(o, i_, *waits):
            return put("dve", lambda e: e.tensor_copy(o, i_), *waits)

        def recip(o, i_, *waits):
            return put("dve", lambda e: e.reciprocal(o, i_), *waits)

        def red(o, i_, op, *waits):
            return put("dve", lambda e: e.tensor_reduce(o, i_, AX_X, op), *waits)

        waiting = []
        mod_waiting = []
        early = []
        n_submit = [0]

        def load_piece(src, k):
            rb, wb = raw.next(), whl.next()
            n = k * 128
            t0 = P.dma("sp", rb.ap[:, 0:n], src, rb.free, slot=rb)
            wf, wr = wb.ap
            t1 = act(wr[:, 0:n], rb.ap[:, 0:n], ACT.Copy, t0, wb.free)
            t2 = tt(wr[:, 1024:1024 + n], rb.ap[:, 0:n], wf[:, 0:n], ALU.subtract, t0, t1)
            rb.free = [t2]
            hi = wr[:, 0:n].rearrange("p (k n) -> p k n", k=k)
            lo = wr[:, 1024:1024 + n].rearrange("p (k n) -> p k n", k=k)
            return wb, hi, lo, [t1, t2]

        def run_waiting(n):
            while mod_waiting:
                h, body = mod_waiting.pop(0)
                body(h)
            while len(waiting) > n:
                h, body = waiting.pop(0)
                body(h)

        def submit(load, body):
            n_submit[0] += 1
            waiting.append((early.pop(0) if early else load(), body))
            run_waiting(2)
            mod_finish()
            mod_credit[0] += mod_rate[0]
            if mod_credit[0] >= 1:
                mod_credit[0] -= 1
                mod_step()

        def piece(src, k=8):
            def load_w():
                return load_piece(src, k)
            return load_w

        def prefetch(*srcs):
            run_waiting(0)
            assert not early
            for src in srcs:
                early.append(load_piece(src, 8))

        def gemm(o, w, rhs, k0, toks, waits, start=True, stop=True):
            wb, hi, lo, tw = w
            k = hi.shape[1]
            for i in range(k):
                a, b = rhs(k0 + i)
                tok = mm(o, [(hi[:, i, :], a), (hi[:, i, :], b), (lo[:, i, :], a)],
                         (tw + waits) if i == 0 else None, toks[k0 + i] if toks else None,
                         start=start and i == 0, stop=stop and i == k - 1)
            wb.free = [tok]
            return tok

        def split(hi_r, hi_f, lo_r, src, *waits):
            t1 = act(hi_r, src, ACT.Copy, *waits)
            return tt(lo_r, src, hi_f, ALU.subtract, t1)

        hrhs = lambda k: (hhr[:, k, :], hlr[:, k, :])

        t_col = P.dma("act", col, t["cols"])
        t_const = P.dma("act", const.rearrange("p a n -> p (a n)"), t["consts"])
        t_x0 = P.dma("act", xT.rearrange("p k n -> p (k n)"), t["xT"])
        xtok = [[t_x0] for _ in range(8)]

        t_c = act(csil[:, 0:8], cc("c", 0, 8), ACT.Silu, t_col)
        t_c = act(csil[:, 8:16], cc("c2", 0, 8), ACT.Silu, t_col)
        mod_tok = [None] * 36
        pending = [(j, p) for j in range(36) for p in range(4)]
        mod_credit, mod_rate = [0.0], [0.8]
        mod_st = {}
        mod_late = []
        lof = hf[:, 4096:8192]
        first = Ring(raw.banks + [Bank(lof[:, 1024 * i:1024 * i + 1024], P.new_sem()) for i in range(4)])

        def mod_step():
            if not pending:
                return
            j, p = pending.pop(0)
            src = t["ada"][j] if j < 24 else t["ada2"][j - 24]
            c0 = 0 if j < 24 else 8
            rb = (first if j < 4 else raw).next()
            load = P.dma("sp", rb.ap, src[:, 1024 * p:1024 * p + 1024], rb.free, slot=rb)

            def body(tok):
                if p == 0:
                    mod_st["acc"] = macc.next()
                acc = mod_st["acc"]
                for i in range(2):
                    ck = csil[:, c0 + 2 * p + i:c0 + 2 * p + i + 1]
                    w = rb.ap[:, 512 * i:512 * i + 512]
                    if p == 0 and i == 0:
                        mod_st["t"] = ts(acc.ap, w, ck, ALU.mult, tok, t_c, acc.free)
                    else:
                        mod_st["t"] = stt(acc.ap, w, ck, acc.ap, ALU.mult, ALU.add, tok, mod_st["t"])
                rb.free = [mod_st["t"]]
                if p == 3:
                    mod_late.append((n_submit[0] + 3, j, acc, mod_st["t"]))
            mod_waiting.append((load, body))

        def mod_finish(force=False):
            while mod_late and (force or mod_late[0][0] <= n_submit[0]):
                _, j, acc, t0 = mod_late.pop(0)
                bank = ring.next()
                for m in range(4):
                    tok = mm(bank.ap[:, m:m + 1], [(acc.ap[:, 128 * m:128 * m + 128], ones[:, 0:1])],
                             t0, t_const, bank.free)
                acc.free = [tok]
                o = 4 * j
                bias = cc("adab", o, 4) if j < 24 else cc("adab2", o - 96, 4)
                mod_tok[j] = tt(mod[:, o:o + 4], bank.ap[:, 0:4], bias, ALU.add, tok, t_col)
                bank.free = [mod_tok[j]]

        def mods_until(j):
            while pending and pending[0][0] <= j:
                mod_step()
                run_waiting(2)
                if len(mod_late) > 1:
                    mod_finish(True)
            run_waiting(0)
            mod_finish(True)

        def derived(i):
            j0 = 6 * i
            mods_until(j0 + 3)
            o = 24 * i
            g_pre = cc("ng", 16 * i, 8) if i < 4 else cc("n1" if i == 4 else "n2", 0, 8)
            return stt(der[:, o:o + 8], mod[:, o + 8:o + 16], 1.0, g_pre, ALU.add, ALU.mult,
                       mod_tok[j0:j0 + 4], t_col)

        def derived_post(i):
            j0 = 6 * i
            mods_until(j0 + 5)
            o = 24 * i
            if i < 4:
                return tt(der[:, o + 8:o + 16], mod[:, o + 16:o + 24], cc("ng", 16 * i + 8, 8), ALU.mult,
                          mod_tok[j0 + 4:j0 + 6], t_col)
            return vcopy(der[:, o + 8:o + 16], mod[:, o + 16:o + 24], mod_tok[j0 + 4:j0 + 6])

        def shift(i, k):
            return mod[:, 24 * i + k:24 * i + k + 1]

        def pre(i, k):
            return der[:, 24 * i + k:24 * i + k + 1]

        def post(i, k):
            return der[:, 24 * i + 8 + k:24 * i + 9 + k]

        def sq_stat(bank, src, k, n, mat, *waits):
            b = tmp.next()
            t1 = act(b.ap, src, ACT.Square, b.free, *waits)
            t2 = mm(bank.ap, [(mat, b.ap)], t1, t_const, bank.free if k == 0 else None,
                    start=k == 0, stop=k == n - 1)
            b.free = [t2]
            return t1, t2

        def rstd(bank, tok, n, dst=None, dfree=None):
            if dst is None:
                r = rst.next()
                dst, dfree = r.ap, r.free
            else:
                r = None
            t0 = ts(dst, bank.ap, 1.0 / n, ALU.mult, tok, dfree, s2=EPS, op1=ALU.add)
            bank.free = [t0]
            t1 = act(dst, dst, ACT.Ln, t0)
            t2 = act(dst, dst, ACT.Exp, t1, scale=-0.5)
            return r, dst, t2

        h_free = [[] for _ in range(8)]

        def pre_norm(i, t_sh):
            bank = ring.next()
            for k in range(8):
                _, tok = sq_stat(bank, xT[:, k, :], k, 8, ones, xtok[k])
            r, ra, tr_ = rstd(bank, tok, D)
            toks = []
            made = []
            for k in range(10):
                if k < 8:
                    b = tmp.next()
                    t1 = stt(b.ap, xT[:, k, :], pre(i, k), ra, ALU.mult, ALU.mult, tr_, t_sh, xtok[k], b.free)
                    t2 = act(hhr[:, k, :], b.ap, ACT.Identity, t1, h_free[k], bias=shift(i, k))
                    made.append((b, t2))
                if k > 1:
                    b, t2 = made[k - 2]
                    t3 = stt(hlr[:, k - 2, :], b.ap, shift(i, k - 2), hhf[:, k - 2, :], ALU.add, ALU.subtract, t2,
                             h_free[k - 2])
                    b.free = [t3]
                    toks.append(t3)
            r.free = [t1]
            return toks

        def out_proj(src, kgroups, rhs, rhs_tok, norm=True, half=None):
            nonlocal ring
            ring_keep = ring
            ring = ring7
            stat = banks[7]
            yT = k8(hf[:, 0:4096])
            st_ = {"pend": None}
            t_post = None if norm else derived_post(half)
            for kk in range(8):
                for si, (k0, nk) in enumerate(kgroups):
                    last = si == len(kgroups) - 1

                    def body(w, kk=kk, si=si, k0=k0, nk=nk, last=last):
                        if si == 0:
                            st_["bk"] = ring.next()
                        bk = st_["bk"]
                        tok = gemm(bk.ap, w, rhs, k0, rhs_tok, bk.free if si == 0 else [],
                                   start=si == 0, stop=last)
                        if not last:
                            return
                        if not norm:
                            t1 = stt(xT[:, kk, :], bk.ap, post(half, kk), xT[:, kk, :], ALU.mult, ALU.add,
                                     tok, t_post, xtok[kk])
                            bk.free = [t1]
                            xtok[kk] = [t1]
                            return
                        t1 = act(yT[:, kk, :], bk.ap, ACT.Copy, tok, h_free[kk])
                        sb = tmp.next()
                        t2 = act(sb.ap, bk.ap, ACT.Square, sb.free, tok)
                        bk.free = [t1, t2]
                        ytok[kk] = t1
                        if st_["pend"]:
                            st_["pend"]()

                        def pend():
                            t3 = mm(stat.ap, [(ones, sb.ap)], t2, stat.free if kk == 0 else None,
                                    start=kk == 0, stop=kk == 7)
                            sb.free = [t3]
                            return t3
                        st_["pend"] = pend
                    submit(piece(src[kk, :, k0 * 128:(k0 + nk) * 128], nk), body)
            if norm:
                t_post = derived_post(half)
            run_waiting(0)
            ring = ring_keep
            if norm:
                tok = st_["pend"]()
                r, ra, tr_ = rstd(stat, tok, D)
                for k in range(8):
                    b = tmp.next()
                    t1 = stt(b.ap, yT[:, k, :], post(half, k), ra, ALU.mult, ALU.mult, tr_, t_post, ytok[k], b.free)
                    t2 = tt(xT[:, k, :], xT[:, k, :], b.ap, ALU.add, t1, xtok[k], eng="pool" if k % 3 == 2 else "dve")
                    b.free = [t2]
                    xtok[k] = [t2]
                    h_free[k] = [t1]
                r.free = [t1]

        ytok = [None] * 8
        ring7 = Ring(banks[0:7])

        region_free = []

        def ffn(layer, half):
            at[0] = BASE
            ahf, ahr = [a.rearrange("p (k n) -> p k n", k=KF) for a in take_r(KF * 512)]
            alf, alr = [a.rearrange("p (k n) -> p k n", k=KF) for a in take_r(KF * 512)]
            t_pre = derived(half)
            prefetch(t["fin"][layer, 0], t["fin"][layer, 1])
            ht = pre_norm(half, t_pre)
            atok = [None] * KF
            st_ = {}
            for kk in range(KF):
                def body_g(w, kk=kk):
                    bg = ring.next()
                    tg = gemm(bg.ap, w, hrhs, 0, ht, bg.free)
                    sb = tmp.next()
                    t1 = act(sb.ap, bg.ap, ACT.Silu, tg, sb.free)
                    bg.free = [t1]
                    st_["g"] = sb, t1

                def body_u(w, kk=kk):
                    sb, t1 = st_["g"]
                    bu = ring.next()
                    tu = gemm(bu.ap, w, hrhs, 0, None, bu.free)
                    t2 = tt(sb.ap, bu.ap, sb.ap, ALU.mult, tu, t1)
                    bu.free = [t2]
                    atok[kk] = split(ahr[:, kk, :], ahf[:, kk, :], alr[:, kk, :], sb.ap, t2, region_free)
                    sb.free = [atok[kk]]
                    st_["u"] = tu
                submit(piece(t["fin"][layer, 2 * kk]), body_g)
                submit(piece(t["fin"][layer, 2 * kk + 1]), body_u)
            run_waiting(0)
            for k in range(8):
                h_free[k] = [st_["u"]]
            out_proj(t["fout"][layer], [(0, 8), (8, 8), (16, 6)], lambda k: (ahr[:, k, :], alr[:, k, :]), atok,
                     True, half)
            region_free[:] = list(h_free[0])

        def conv_mixer():
            at[0] = BASE
            uhf, uhr = [k8(a) for a in take_r(4096)]
            ulf, ulr = [k8(a) for a in take_r(4096)]
            vb = Ring([Bank(take(512)) for _ in range(3)])
            t_pre = derived(0)
            prefetch(t["ain"][0], t["ain"][8])
            for k in range(8):
                h_free[k] = [x for b in first.banks[4:] for x in b.free]
            ht = pre_norm(0, t_pre)
            ut = [None] * 8
            st_ = {}
            cw = COL["acw"]
            for kk in range(8):
                def body_c(w, kk=kk):
                    bk, v = ring.next(), vb.next()
                    tok = gemm(bk.ap, w, hrhs, 0, ht, bk.free)
                    t1 = act(v.ap, bk.ap, ACT.Copy, tok, v.free)
                    bk.free = [t1]
                    st_["v"] = v, t1

                def body_v(w, kk=kk):
                    v, t1 = st_["v"]
                    bk = ring.next()
                    tok = gemm(bk.ap, w, hrhs, 0, None, bk.free)
                    t1 = tt(v.ap, bk.ap, v.ap, ALU.mult, tok, t1)
                    bk.free = [t1]
                    u = tmp.next()
                    t2 = act(u.ap, v.ap, ACT.Copy, t1, u.free, scale=col[:, cw + 16 + kk:cw + 17 + kk])
                    for tap, d in ((1, 1), (0, 2)):
                        t2 = stt(u.ap[:, d:512], v.ap[:, 0:512 - d], col[:, cw + 8 * tap + kk:cw + 8 * tap + kk + 1],
                                 u.ap[:, d:512], ALU.mult, ALU.add, t2)
                    v.free = [t2]
                    st_["u"] = u, t2

                def body_b(w, kk=kk):
                    u, t2 = st_["u"]
                    bk = ring.next()
                    tok = gemm(bk.ap, w, hrhs, 0, None, bk.free)
                    t3 = tt(u.ap, bk.ap, u.ap, ALU.mult, tok, t2)
                    bk.free = [t3]
                    ut[kk] = split(uhr[:, kk, :], uhf[:, kk, :], ulr[:, kk, :], u.ap, t3)
                    u.free = [ut[kk]]
                    st_["last"] = tok
                submit(piece(t["ain"][kk]), body_c)
                submit(piece(t["ain"][8 + kk]), body_v)
                submit(piece(t["ain"][16 + kk]), body_b)
            run_waiting(0)
            for k in range(8):
                h_free[k] = [st_["last"]]
            out_proj(t["aout"], [(0, 8)], lambda k: (uhr[:, k, :], ulr[:, k, :]), ut, True, 0)
            region_free[:] = list(h_free[0])
            mod_rate[0] = 0.5

        def conv4(src_bank, dst, wcol, kk, ncol, tok, *waits, bias=None):
            w = lambda tap: col[:, wcol + ncol * tap + kk:wcol + ncol * tap + kk + 1]
            sb = tmp.next()
            if bias is None:
                t1 = act(sb.ap, src_bank.ap, ACT.Copy, tok, sb.free, scale=w(3))
            else:
                t1 = act(sb.ap, src_bank.ap, ACT.Identity, tok, sb.free, scale=w(3), bias=bias)
            for tap, d in ((2, 1), (1, 2), (0, 3)):
                t1 = stt(sb.ap[:, d:512], src_bank.ap[:, 0:512 - d], w(tap), sb.ap[:, d:512], ALU.mult, ALU.add, t1)
            src_bank.free = [t1]
            t2 = act(dst, sb.ap, ACT.Silu, t1, *waits)
            sb.free = [t2]
            return t2

        def softplus(dst, tmp3, *waits):
            e, u, v = tmp3
            t1 = act(e, dst, ACT.Abs, *waits)
            t2 = act(e, e, ACT.Exp, t1, scale=-1.0)
            t3 = ts(u, e, 2.0, ALU.add, t2)
            t4 = recip(u, u, t3)
            t5 = tt(e, e, u, ALU.mult, t4)
            t6 = tt(u, e, e, ALU.mult, t5)
            t7 = ts(v, u, 1.0 / 17.0, ALU.mult, t6)
            for n in (15, 13, 11, 9, 7, 5, 3):
                t7 = stt(v, v, 1.0 / n, u, ALU.add, ALU.mult, t7)
            t8 = stt(v, v, 1.0, e, ALU.add, ALU.mult, t7)
            t9 = ts(v, v, 2.0, ALU.mult, t8)
            return stt(dst, dst, 0.0, v, ALU.max, ALU.add, t9)

        def ssd_mixer():
            nonlocal ring
            at[0] = BASE
            xs_at = at[0]
            xs = take(16 * 512).rearrange("p (k n) -> p k n", k=16)
            hi_at = at[0]
            BT = take(8 * 512).rearrange("p (k n) -> p k n", k=8)
            CT = take(8 * 512).rearrange("p (k n) -> p k n", k=8)
            sp3 = [tmp.next() for _ in range(3)]
            dttok = take(128).rearrange("p (c h) -> p c h", c=4)
            datok = take(128).rearrange("p (c h) -> p c h", c=4)
            cstok = take(128).rearrange("p (c h) -> p c h", c=4)
            wtok = take(128).rearrange("p (c h) -> p c h", c=4)
            cdec = take(128).rearrange("p (c h) -> p c h", c=4)
            nega = take(1)
            segb = [Bank(take(512)) for _ in range(3)]
            dtT, daT = [b.ap[0:32, :] for b in segb[0:2]]
            ceb = [Bank(take(512)) for _ in range(3)]
            cbm = [Bank(take(128)) for _ in range(3)]
            xdt = [Bank(take(256)) for _ in range(3)]
            xw = [Bank(take(256)) for _ in range(3)]
            btk = [Bank(take(128)) for _ in range(3)]
            st = [Bank(take(256)) for _ in range(2)]
            t_pre = derived(2)
            prefetch(t["mdt"], t["mxbc"][0])
            ht = pre_norm(2, t_pre)

            bk = ring.next()
            box = {}
            submit(piece(t["mdt"]), lambda w: box.update(t=gemm(bk.ap, w, hrhs, 0, ht, bk.free)))
            run_waiting(0)
            tok = box["t"]
            t1 = act(dtT, bk.ap[0:32, :], ACT.Identity, tok, region_free, bias=cc("mdt")[0:32, :])
            bk.free = [t1]
            ta = act(nega[0:32, :], cc("mal")[0:32, :], ACT.Exp, region_free, t_col)
            ta = ts(nega[0:32, :], nega[0:32, :], -1.0, ALU.mult, ta)
            t2 = softplus(dtT, [s.ap[0:32, :] for s in sp3], t1, *[s.free for s in sp3])
            for s in sp3:
                s.free = [t2]
            t3 = ts(daT, dtT, nega[0:32, 0:1], ALU.mult, t2, ta, region_free)
            bk = ring.next()
            bk2 = ring.next()
            for c in range(4):
                q1 = tr(bk.ap[:, 32 * c:32 * c + 32], dtT[:, 128 * c:128 * c + 128], 32, t2, bk.free, t_const)
                q2 = tr(bk2.ap[:, 32 * c:32 * c + 32], daT[:, 128 * c:128 * c + 128], 32, t3, bk2.free)
            flat = lambda a: a.rearrange("p c h -> p (c h)")
            d1 = act(flat(dttok), bk.ap[:, 0:128], ACT.Copy, q1, region_free)
            d2 = act(flat(datok), bk2.ap[:, 0:128], ACT.Copy, q2, region_free)
            bk.free, bk2.free = [d1], [d2]
            segb[0].free, segb[1].free = [q2], [q2]
            b1, b2 = ring.next(), ring.next()
            q1 = mm(b1.ap[:, 0:128], [(tri, flat(datok))], d2, b1.free)
            q2 = mm(b2.ap[:, 0:128], [(ones, flat(datok))], d2, b2.free)
            q2 = mm(b2.ap[:, 128:256], [(gt_, flat(datok))])
            d3 = act(flat(cstok), b1.ap[:, 0:128], ACT.Copy, q1, region_free)
            d5 = act(flat(cdec), b2.ap[:, 0:128], ACT.Exp, q2, region_free)
            d4 = act(flat(wtok), b2.ap[:, 128:256], ACT.Exp, q2, region_free)
            b1.free, b2.free = [d3], [d4]

            tk = {}
            for n in range(32):
                def body(w, n=n):
                    dst, ct = (BT[:, n, :], 16 + n) if n < 8 else (CT[:, n - 8, :], 16 + n) if n < 16 else (xs[:, n - 16, :], n - 16)
                    bk = ring.next()
                    tok = gemm(bk.ap, w, hrhs, 0, None, bk.free)
                    tk[n] = conv4(bk, dst, COL["mcw"], ct, 32, tok, region_free, bias=cc("mcb", ct))
                submit(piece(t["mxbc"][n]), body)
            run_waiting(0)

            yb = [[banks[0], banks[1]], [banks[0], banks[1]]]
            ring_keep = ring
            ring = Ring(banks[2:4])
            rg = Ring(banks[4:8])
            state = {}
            its = [(g, c) for g in range(8) for c in range(4)]

            def stage_a(n):
                g, c = its[n]
                p = n % 3
                cs = slice(128 * c, 128 * c + 128)
                s = {}
                b1, b2 = rg.next(), rg.next()
                q1 = mm(b1.ap[:, 0:128], [(BT[:, g, cs], CT[:, g, cs])], tk[g], tk[8 + g], b1.free)
                for r in range(4):
                    q2 = mm(b2.ap[:, 128 * r:128 * r + 128],
                            [(datok[:, c, 4 * g + r:4 * g + r + 1].broadcast_to([128, 128]), tri)], d2, b2.free)
                q3 = tr(b1.ap[:, 128:256], BT[:, g, cs], 128, q1)
                for u in range(2):
                    q4 = tr(b1.ap[:, 256 + 128 * u:384 + 128 * u], xs[:, 2 * g + u, cs], 128, tk[16 + 2 * g + u])
                yield
                s["cbm"] = tt(cbm[p].ap, b1.ap[:, 0:128], tri, ALU.mult, q4, cbm[p].free)
                v = segb[p].ap.rearrange("p (r n) -> p r n", r=4)
                hs = slice(4 * g, 4 * g + 4)
                t1 = tt(v, b2.ap.rearrange("p (r n) -> p r n", r=4),
                        cstok[:, c, hs].unsqueeze(2).broadcast_to([128, 4, 128]), ALU.subtract, q2, d3, segb[p].free)
                t2 = ts(segb[p].ap, segb[p].ap, 0.0, ALU.min, t1)
                t3 = act(ceb[p].ap, b2.ap, ACT.Exp, q2, t1, ceb[p].free)
                b2.free = [t1, t3]
                s["e"] = act(segb[p].ap, segb[p].ap, ACT.Exp, t2)
                x4 = xdt[p].ap.rearrange("p (r n) -> p r n", r=4)
                s["xdt"] = tt(x4, b1.ap[:, 256:512].rearrange("p (r n) -> p r n", r=4),
                              dttok[:, c, hs].unsqueeze(2).broadcast_to([128, 4, 64]), ALU.mult, q4, d1, xdt[p].free)
                s["btk"] = act(btk[p].ap, b1.ap[:, 128:256], ACT.Copy, q3, s["xdt"], btk[p].free)
                b1.free = [s["cbm"], s["xdt"], s["btk"]]
                ce = ceb[p].ap.rearrange("p (r n) -> p r n", r=4)
                if c:
                    s["ce"] = tt(ce, ce, CT[:, g, cs].unsqueeze(1).broadcast_to([128, 4, 128]), ALU.mult, t3)
                if c < 3:
                    xwv = xw[p].ap.rearrange("p (r n) -> p r n", r=4)
                    s["xw"] = tt(xwv, x4, wtok[:, c, hs].unsqueeze(2).broadcast_to([128, 4, 64]), ALU.mult,
                                 s["xdt"], d4, xw[p].free, eng="pool")
                else:
                    s["xw"] = None
                state[n] = s

            def stage_b(n):
                g, c = its[n]
                p = n % 3
                s = state.pop(n)
                cs = slice(128 * c, 128 * c + 128)
                v = segb[p].ap.rearrange("p (r n) -> p r n", r=4)
                tg = tt(v, v, cbm[p].ap.unsqueeze(1).broadcast_to([128, 4, 128]), ALU.mult, s["e"], s["cbm"])
                cbm[p].free = [tg]
                prev = st[g % 2]
                y = yb[g % 2]
                for r in range(4):
                    u, o = r // 2, 64 * (r % 2)
                    pairs = [(xdt[p].ap[:, 64 * r:64 * r + 64], v[:, r, :])]
                    if c:
                        pairs.append((prev.ap[:, 64 * r:64 * r + 64], ceb[p].ap[:, 128 * r:128 * r + 128]))
                    q = mm(y[u].ap[o:o + 64, cs], pairs, tg, s["xdt"], s.get("ce"), prev.tok if c else None,
                           y[u].free if c == 0 else None)
                segb[p].free = [q]
                ceb[p].free = [q]
                xdt[p].free = [q, s["xw"]] if s["xw"] else [q]
                if c == 0:
                    btkw = prev.free
                if c < 3:
                    b3 = rg.next()
                    q2 = mm(b3.ap[:, 0:256], [(btk[p].ap, xw[p].ap)], s["btk"], s["xw"], b3.free)
                    xw[p].free = [q2]
                    btk[p].free = [q2]
                    pv = prev.ap.rearrange("p (r n) -> p r n", r=4)
                    if c == 0:
                        prev.tok = act(prev.ap, b3.ap[:, 0:256], ACT.Copy, q2, btkw)
                    else:
                        t1 = tt(pv, pv, cdec[:, c, 4 * g:4 * g + 4].unsqueeze(2).broadcast_to([128, 4, 64]), ALU.mult,
                                d5, prev.tok, q)
                        prev.tok = tt(prev.ap, b3.ap[:, 0:256], prev.ap, ALU.add, q2, t1)
                    b3.free = [prev.tok]
                else:
                    btk[p].free = [s["btk"]]
                    prev.free = [q]
                    for u in range(2):
                        kk = 2 * g + u
                        tk[16 + kk] = stt(xs[:, kk, :], xs[:, kk, :], cc("md", kk), y[u].ap, ALU.mult, ALU.add, q, tk[16 + kk])
                        y[u].free = [tk[16 + kk]]

            gt = [None] * 16
            box = {}

            def norm_pair(g):
                bk = ring.next()
                for u in range(2):
                    _, tq = sq_stat(bk, xs[:, 2 * g + u, :], u, 2, ones, gt[2 * g + u])
                r, ra, tr_ = rstd(bk, tq, 256)
                for u in range(2):
                    kk = 2 * g + u
                    gt[kk] = stt(xs[:, kk, :], xs[:, kk, :], cc("mng", kk), ra, ALU.mult, ALU.mult, tr_, gt[kk])
                r.free = [gt[2 * g + 1]]

            def submit_z(kk):
                def body(w):
                    bk = ring.next()
                    tok = gemm(bk.ap, w, hrhs, 0, None, bk.free)
                    sb = tmp.next()
                    t1 = act(sb.ap, bk.ap, ACT.Silu, tok, sb.free)
                    bk.free = [t1]
                    gt[kk] = tt(xs[:, kk, :], xs[:, kk, :], sb.ap, ALU.mult, t1, tk[16 + kk])
                    sb.free = [gt[kk]]
                    if kk % 2 == 0 and kk:
                        norm_pair(kk // 2 - 1)
                    box["t"] = tok
                submit(piece(t["mz"][kk]), body)

            for n in range(len(its) + 2):
                a_ = stage_a(n) if n < len(its) else iter(())
                next(a_, None)
                if n > 1:
                    stage_b(n - 2)
                next(a_, None)
                if 4 < n < 33 and n % 2:
                    submit_z((n - 5) // 2)
            submit_z(14)
            submit_z(15)
            run_waiting(0)
            ring = ring_keep
            norm_pair(7)
            at[0] = hi_at
            ohf, ohr = [a.rearrange("p (k n) -> p k n", k=16) for a in take_r(8192)]
            olr = take_r(8192, xs_at)[1].rearrange("p (k n) -> p k n", k=16)
            for kk in range(16):
                gt[kk] = split(ohr[:, kk, :], ohf[:, kk, :], olr[:, kk, :], xs[:, kk, :], gt[kk], tk[31])
            for k in range(8):
                h_free[k] = [box["t"]]
            out_proj(t["mout"], [(0, 8), (8, 8)], lambda k: (ohr[:, k, :], olr[:, k, :]), gt, True, 2)
            region_free[:] = list(h_free[0])

        def hybrid():
            nonlocal ring
            at[0] = BASE
            t_pre = derived(4)
            prefetch(t["win2"][0], t["win2"][1])
            ht = pre_norm(4, t_pre)
            mix_at = at[0]
            mix = take(4096).rearrange("p (k n) -> p k n", k=8)
            mark = at[0]
            qT = take(2048).rearrange("p (k n) -> p k n", k=4)
            kT = take(2048).rearrange("p (k n) -> p k n", k=4)
            vtok = take(2048).rearrange("p (k n) -> p k n", k=4)
            T = take(4096).rearrange("p (h n) -> p h n", h=8)
            Sb = [Bank(take(512)) for _ in range(3)]
            PT = [Bank(take(2048).rearrange("p (j n) -> p j n", j=4)) for _ in range(2)]
            sm = [Bank(take(4)) for _ in range(4)]
            t_T = P.dma("act", T.rearrange("p h n -> p (h n)"), t["relT"], region_free)
            t_T = put("dve", lambda e: e.memset(T[0:64, :, 448:512], -3.0e38), t_T)

            def rows(bk, tok, kk, dst, gain):
                t0 = act(dst, bk.ap, ACT.Copy, tok, region_free)
                bk2 = ring.next()
                sb = tmp.next()
                t1 = act(sb.ap, bk.ap, ACT.Square, sb.free, tok)
                bk.free = [t0, t1]
                t2 = mm(bk2.ap, [(blk, sb.ap)], t1, bk2.free)
                sb.free = [t2]
                r, ra, tr_ = rstd(bk2, t2, 64)
                t3 = stt(dst, dst, gain, ra, ALU.mult, ALU.mult, tr_, t0)
                r.free = [t3]
                return t3

            qt, kt = [None] * 4, [None] * 4
            vt = [None] * 4
            for n in range(12):
                def body(w, n=n):
                    bk = ring.next()
                    tok = gemm(bk.ap, w, hrhs, 0, ht, bk.free)
                    m = n % 4
                    if n < 8:
                        dst, toks, gain = ((qT, qt, cc("qg")), (kT, kt, cc("kg")))[n // 4]
                        toks[m] = rows(bk, tok, m, dst[:, m, :], gain)
                        return
                    sb = tmp.next()
                    t1 = act(sb.ap, bk.ap, ACT.Copy, tok, sb.free)
                    bk.free = [t1]
                    bk2 = ring.next()
                    for c in range(4):
                        q = tr(bk2.ap[:, 128 * c:128 * c + 128], sb.ap[:, 128 * c:128 * c + 128], 128, t1, bk2.free)
                    sb.free = [q]
                    vt[m] = act(vtok[:, :, 128 * m:128 * m + 128], bk2.ap.rearrange("p (c n) -> p c n", c=4), ACT.Copy,
                                q, region_free)
                    bk2.free = [vt[m]]
                submit(piece(t["win2"][n]), body)
            run_waiting(0)

            ring_keep = ring
            ring = Ring(banks[0:6])
            its = [(h, i) for h in range(8) for i in range(4)]
            state = {}

            def att_a(n):
                h, i = its[n]
                L = 128 * (i + 1)
                o = 64 * (h % 2)
                bk = ring.next()
                q = mm(bk.ap[:, 0:L], [(qT[o:o + 64, h // 2, 128 * i:128 * i + 128], kT[o:o + 64, h // 2, 0:L])],
                       qt[h // 2], kt[h // 2], bk.free)
                yield
                sb = Sb[n % 3]
                s4 = sm[n % 4]
                t1 = stt(sb.ap[:, 0:L], bk.ap[:, 0:L], 0.125, T[:, h, 512 - L:512], ALU.mult, ALU.add,
                         q, t_T, sb.free)
                bk.free = [t1]
                t2 = red(s4.ap[:, 0:1], sb.ap[:, 0:L], ALU.max, t1, s4.free)
                t2 = ts(s4.ap[:, 1:2], s4.ap[:, 0:1], -1.0, ALU.mult, t2)
                t3 = act(sb.ap[:, 0:L], sb.ap[:, 0:L], ACT.Exp, t2, bias=s4.ap[:, 1:2], accum=s4.ap[:, 2:3])
                state[n] = t3

            def att_b(n):
                h, i = its[n]
                L = 128 * (i + 1)
                sb = Sb[n % 3]
                s4 = sm[n % 4]
                t3 = state.pop(n)
                t4 = recip(s4.ap[:, 3:4], s4.ap[:, 2:3], t3)
                t5 = ts(sb.ap[:, 0:L], sb.ap[:, 0:L], s4.ap[:, 3:4], ALU.mult, t4)
                s4.free = [t5]
                bk = ring.next()
                for j in range(i + 1):
                    q = tr(bk.ap[:, 128 * j:128 * j + 128], sb.ap[:, 128 * j:128 * j + 128], 128, t5, bk.free)
                sb.free = [q]
                pt = PT[h % 2]
                t6 = act(pt.ap[:, 0:i + 1, 128 * i:128 * i + 128], bk.ap[:, 0:L].rearrange("p (j n) -> p j n", n=128),
                         ACT.Copy, q, pt.free if i == 0 else None)
                bk.free = [t6]
                if i == 3:
                    o = 64 * (h % 2)
                    bo = banks[6 + h // 2 % 2]
                    for j in range(4):
                        q = mm(bo.ap[o:o + 64, 128 * j:512], [(vtok[:, j, 64 * h:64 * h + 64], pt.ap[:, j, 128 * j:512])],
                               t6, vt[h // 2], bo.free, start=j == 0, stop=j == 3)
                    pt.free = [q]
                    if h % 2:
                        att_tok[h // 2] = act(mix[:, h // 2, :], bo.ap, ACT.Copy, q)
                        bo.free = [att_tok[h // 2]]

            att_tok = [None] * 4
            for n in range(len(its) + 2):
                a_ = att_a(n) if n < len(its) else iter(())
                next(a_, None)
                if n > 1:
                    att_b(n - 2)
                next(a_, None)
            ring = ring_keep
            bk = ring.next()
            for k in range(4):
                _, tok = sq_stat(bk, mix[:, k, :], k, 4, ones, att_tok[k])
            r, ra, tr_ = rstd(bk, tok, 512)
            mt = [None] * 8
            for k in range(4):
                mt[k] = stt(mix[:, k, :], mix[:, k, :], cc("aog", k), ra, ALU.mult, ALU.mult, tr_, att_tok[k])
            r.free = [mt[3]]
            aft = [mt[3]]

            at[0] = mark
            Q = take(2048).rearrange("p (k n) -> p k n", k=4)
            K = take(2048).rearrange("p (k n) -> p k n", k=4)
            V = take(2048).rearrange("p (k n) -> p k n", k=4)
            GB = take(2048).rearrange("p (k n) -> p k n", k=4)
            Vtk = take(2048).rearrange("p (c n) -> p c n", c=4)
            Ktk = take(2048).rearrange("p (c n) -> p c n", c=4)
            bg_ = take(512)
            bT, gT = bg_[0:4, :], bg_[32:36, :]
            btok = take(16).rearrange("p (c h) -> p c h", c=4)
            gtok = take(16).rearrange("p (c h) -> p c h", c=4)
            eg = take(16).rearrange("p (c h) -> p c h", c=4)
            eb = take(16).rearrange("p (c h) -> p c h", c=4)
            wk = take(16).rearrange("p (c h) -> p c h", c=4)
            gl = take(16).rearrange("p (c h) -> p c h", c=4)
            nega = take(1)
            lvl = take(896).rearrange("p (a n) -> p a n", a=7)
            t_lvl = P.dma("sp", lvl.rearrange("p a n -> p (a n)"), t["levels"], aft)
            spare = tmp.banks
            Lts = [Bank(take(512)), spare[0]]
            Xbs = [Bank(take(512)), spare[1]]
            Dbs = [Bank(take(512)), spare[2]]
            dcys = [Bank(take(512)), spare[3]]
            At = [Bank(take(512)), Bank(take(512)), spare[4], spare[5]]
            DTb = [Bank(take(512)), Bank(take(512)), spare[6], spare[7]]
            Sst = Bank(take(512))
            assert not pending and not mod_late
            Rb, Vn = macc.banks
            v4 = lambda a: a.rearrange("p (h n) -> p h n", h=4)
            fl = lambda a: a.rearrange("p c h -> p (c h)")
            bc = lambda a, n=128: a.unsqueeze(2).broadcast_to([128, 4, n])

            bkb = ring.next()
            box = {}
            submit(piece(t["win2ba"]), lambda w: box.update(t=gemm(bkb.ap, w, hrhs, 0, None, bkb.free)))
            run_waiting(0)
            t_b = act(bT, bkb.ap[0:4, :], ACT.Sigmoid, box["t"], aft)
            t1 = act(gT, bkb.ap[32:36, :], ACT.Identity, t_b, aft, bias=cc("ddt")[32:36, :])
            bkb.free = [t1]
            tn = act(nega[32:36, :], cc("dal")[32:36, :], ACT.Exp, aft)
            tn = ts(nega[32:36, :], nega[32:36, :], -1.0, ALU.mult, tn)
            sp3 = [tmp.next() for _ in range(3)]
            t2 = softplus(gT, [s.ap[32:36, :] for s in sp3], t1, *[s.free for s in sp3])
            for s in sp3:
                s.free = [t2]
            t3 = ts(gT, gT, nega[32:36, 0:1], ALU.mult, t2, tn)
            bk, bk2 = ring.next(), ring.next()
            for c in range(4):
                q = tr(bk.ap[:, 4 * c:4 * c + 4], bT[:, 128 * c:128 * c + 128], 4, t_b, bk.free)
            for c in range(4):
                q2 = put("pe", lambda e, c=c, bk2=bk2: e.transpose(bk2.ap[:, 4 * c:4 * c + 4],
                                                                   gT[:, 128 * c:128 * c + 128], ident[32:36, 32:36]),
                         t3, bk2.free)
            e1 = act(fl(btok), bk.ap[:, 0:16], ACT.Copy, q, aft)
            e2 = act(fl(gtok), bk2.ap[:, 0:16], ACT.Copy, q2, aft)
            bk2.free = [e2]
            bk.free = [e1]
            bk = ring.next()
            q = mm(bk.ap[:, 0:16], [(tri, fl(gtok))], e2, bk.free)
            q2 = mm(bk.ap[:, 16:32], [(ones, fl(gtok))])
            q2 = mm(bk.ap[:, 32:48], [(gt_, fl(gtok))])
            e4 = act(fl(eg), bk.ap[:, 0:16], ACT.Exp, q2, aft)
            e6 = act(fl(wk), bk.ap[:, 32:48], ACT.Exp, aft)
            e7 = act(fl(gl), bk.ap[:, 16:32], ACT.Exp, aft)
            e5 = tt(fl(eb), fl(eg), fl(btok), ALU.mult, e4, e1, aft)
            bk.free = [e7]

            qk = {}
            for n in range(12):
                def body(w, n=n):
                    j, m = n // 4, n % 4
                    dst = (Q, K, V)[j]
                    bk = ring.next()
                    tok = gemm(bk.ap, w, hrhs, 0, None, bk.free)
                    if box.get("norm"):
                        box.pop("norm")()
                    t1 = conv4(bk, dst[:, m, :], COL["dcw"], 4 * j + m, 12, tok, aft)
                    qk[j, m] = t1

                    def norm(t1=t1):
                        bk2 = ring.next()
                        _, tq = sq_stat(bk2, dst[:, m, :], 0, 1, ones, t1)
                        r, ra, tr_ = rstd(bk2, tq, 1.0)
                        qk[j, m] = stt(dst[:, m, :], dst[:, m, :], 128.0 ** -0.5 if j == 0 else 1.0, ra,
                                       ALU.mult, ALU.mult, tr_, t1)
                        r.free = [qk[j, m]]
                    if j < 2:
                        box["norm"] = norm
                submit(piece(t["win2"][12 + n]), body)
            run_waiting(0)
            for c in range(4):
                cs = slice(128 * c, 128 * c + 128)
                bk, bk2 = ring.next(), ring.next()
                for h in range(4):
                    q = tr(bk.ap[:, 128 * h:128 * h + 128], K[:, h, cs], 128, qk[1, h], bk.free)
                    q2 = tr(bk2.ap[:, 128 * h:128 * h + 128], V[:, h, cs], 128, qk[2, h], bk2.free)
                qk["k", c] = tt(v4(Ktk[:, c, :]), v4(bk.ap), bc(wk[:, c, :]), ALU.mult, q, e6, aft)
                qk["v", c] = tt(v4(Vtk[:, c, :]), v4(bk2.ap), bc(btok[:, c, :]), ALU.mult, q2, e1, aft)
                bk.free, bk2.free = [qk["k", c]], [qk["v", c]]
            vfree = [q2]
            for h in range(4):
                bk = ring.next()
                for c in range(4):
                    q = mm(bk.ap[:, 128 * c:128 * c + 128], [(btok[:, c, h:h + 1].broadcast_to([128, 128]), ident)],
                           e1, bk.free)
                qk["kb", h] = tt(V[:, h, :], bk.ap, K[:, h, :], ALU.mult, q, qk[1, h], vfree)
                bk.free = [qk["kb", h]]

            made = {}

            def invert(c):
                cs = slice(128 * c, 128 * c + 128)
                Lt, Xb, Db, dcy = Lts[c % 2], Xbs[c % 2], Dbs[c % 2], dcys[c % 2]
                A_ = At[c]
                tm = tt(v4(dcy.ap), gt_.unsqueeze(1).broadcast_to([128, 4, 128]), bc(gtok[:, c, :]), ALU.mult,
                        e2, t_const, dcy.free, aft)
                bk = ring.next()
                for h in range(4):
                    hs = slice(128 * h, 128 * h + 128)
                    q = mm(bk.ap[:, hs], [(dcy.ap[:, hs], tri)], tm, bk.free)
                t1 = act(dcy.ap, bk.ap, ACT.Exp, q)
                bk.free = [t1]
                yield
                if c:
                    bk = ring.next()
                    for h in range(4):
                        q = mm(bk.ap[:, 128 * h:128 * h + 128], [(gtok[:, c, h:h + 1].broadcast_to([128, 128]), tri)],
                               bk.free)
                    tE = act(GB[:, :, cs], v4(bk.ap), ACT.Exp, q, aft)
                    bk.free = [tE]
                    tE = tt(GB[:, :, cs], GB[:, :, cs], Q[:, :, cs], ALU.mult, tE, [qk[0, h] for h in range(4)])
                else:
                    tE = None
                t1 = tt(v4(dcy.ap), v4(dcy.ap), tri.unsqueeze(1).broadcast_to([128, 4, 128]), ALU.mult, t1)
                yield
                bk, bk2 = ring.next(), ring.next()
                for h in range(4):
                    hs = slice(128 * h, 128 * h + 128)
                    q = mm(bk.ap[:, hs], [(K[:, h, cs], V[:, h, cs])], qk["kb", h], bk.free)
                    q2 = mm(bk2.ap[:, hs], [(K[:, h, cs], Q[:, h, cs])], qk[0, h], bk2.free)
                tA = tt(A_.ap, bk2.ap, dcy.ap, ALU.mult, q2, t1, A_.free, aft)
                tL = tt(Lt.ap, bk.ap, dcy.ap, ALU.mult, q, t1, Lt.free, aft)
                bk.free, bk2.free = [tL], [tA]
                dcy.free = [tL]
                tL = tt(v4(Lt.ap), v4(Lt.ap), tris.unsqueeze(1).broadcast_to([128, 4, 128]), ALU.mult, tL)
                yield
                DT = DTb[c]
                bk = ring.next()
                for h in range(4):
                    hs = slice(128 * h, 128 * h + 128)
                    q = tr(bk.ap[:, hs], Lt.ap[:, hs], 128, tL, bk.free)
                tX = tt(v4(Xb.ap), v4(bk.ap), lvl[:, 0, :].unsqueeze(1).broadcast_to([128, 4, 128]), ALU.mult,
                        q, Xb.free, aft, t_lvl)
                bk.free = [tX]
                idb = ident.unsqueeze(1).broadcast_to([128, 4, 128])
                tD = tt(v4(Db.ap), idb, v4(Xb.ap), ALU.subtract, tX, Db.free, aft)
                bk = ring.next()
                for h in range(4):
                    hs = slice(128 * h, 128 * h + 128)
                    q = mm(bk.ap[:, hs], [(Xb.ap[:, hs], ident)], tX, bk.free)
                tDT = stt(v4(DT.ap), v4(bk.ap), -1.0, idb, ALU.mult, ALU.add, q, DT.free, aft)
                bk.free = [tDT]
                Xb.free = [q, tD]
                yield
                for lev in range(1, 7):
                    last = lev == 6
                    bk = ring.next()
                    for h in range(4):
                        hs = slice(128 * h, 128 * h + 128)
                        q = mm(bk.ap[:, hs], [(Lt.ap[:, hs], Db.ap[:, hs])], tL, tD, bk.free)
                    tX = tt(v4(Xb.ap), v4(bk.ap), lvl[:, lev, :].unsqueeze(1).broadcast_to([128, 4, 128]),
                            ALU.mult, q, Xb.free)
                    bk.free = [tX]
                    if last:
                        Lt.free = [q]
                        Db.free = [q]
                    yield
                    bk, bk2 = ring.next(), ring.next()
                    for h in range(4):
                        hs = slice(128 * h, 128 * h + 128)
                        q2 = mm(bk2.ap[:, hs], [(Xb.ap[:, hs], DT.ap[:, hs])], tX, tDT, bk2.free)
                    if not last:
                        for h in range(4):
                            hs = slice(128 * h, 128 * h + 128)
                            q1 = mm(bk.ap[:, hs], [(DT.ap[:, hs], Xb.ap[:, hs])], tX, tDT, bk.free)
                        tD = tt(Db.ap, Db.ap, bk.ap, ALU.subtract, q1, tD)
                        bk.free = [tD]
                        Xb.free = [q1, q2]
                        tDT = tt(DT.ap, DT.ap, bk2.ap, ALU.subtract, q2, q1)
                    else:
                        Xb.free = [q2]
                        tDT = tt(DT.ap, DT.ap, bk2.ap, ALU.subtract, q2)
                    bk2.free = [tDT]
                    yield
                made[c] = A_, DT, tE, tA, tDT

            def advance(c):
                cs = slice(128 * c, 128 * c + 128)
                A_, DT, tE, tA, tDT = made[c]
                if c:
                    bk = ring.next()
                    for h in range(4):
                        hs = slice(128 * h, 128 * h + 128)
                        q = mm(bk.ap[:, hs], [(K[:, h, cs], Sst.ap[:, hs])], Sst.tok, bk.free)
                    t1 = tt(v4(Rb.ap), v4(bk.ap), bc(eb[:, c, :]), ALU.mult, q, e5, Rb.free)
                    bk.free = [t1]
                    tR = tt(Rb.ap, Vtk[:, c, :], Rb.ap, ALU.subtract, t1, qk["v", c])
                    rsrc = Rb.ap
                else:
                    tR = qk["v", 0]
                    rsrc = Vtk[:, 0, :]
                yield
                bk = ring.next()
                for h in range(4):
                    hs = slice(128 * h, 128 * h + 128)
                    q = mm(bk.ap[:, hs], [(DT.ap[:, hs], rsrc[:, hs])], tDT, tR, bk.free)
                Rb.free = [q]
                DT.free = [q]
                tV = act(Vn.ap, bk.ap, ACT.Copy, q, Vn.free, aft)
                bk.free = [tV]
                yield
                bk = ring.next()
                for h in range(4):
                    hs = slice(128 * h, 128 * h + 128)
                    pairs = [(Vn.ap[:, hs], A_.ap[:, hs])]
                    if c:
                        pairs.append((Sst.ap[:, hs], GB[:, h, cs]))
                    q = mm(bk.ap[:, hs], pairs, tV, tA, tE, bk.free)
                A_.free = [q]
                o_tok = act(mix[:, 4:8, cs], v4(bk.ap), ACT.Copy, q)
                bk.free = [o_tok]
                mt[4 + c] = o_tok
                if c < 3:
                    bk = ring.next()
                    for h in range(4):
                        hs = slice(128 * h, 128 * h + 128)
                        q3 = mm(bk.ap[:, hs], [(Ktk[:, c, hs], Vn.ap[:, hs])], qk["k", c], bk.free)
                    if c == 0:
                        Sst.tok = act(Sst.ap, bk.ap, ACT.Copy, q3, aft)
                    else:
                        t1 = tt(v4(Sst.ap), v4(Sst.ap), bc(gl[:, c, :]), ALU.mult, e7, Sst.tok, q)
                        Sst.tok = tt(Sst.ap, bk.ap, Sst.ap, ALU.add, q3, t1)
                    bk.free = [Sst.tok]
                    Vn.free = [q3]
                else:
                    Vn.free = [q]
                yield

            def alternate(*steps):
                live = list(steps)
                while live:
                    live = [g for g in live if next(g, True) is None]

            def two(a, b):
                yield from a
                yield from b

            alternate(invert(0), invert(1))
            alternate(invert(2), invert(3), two(advance(0), advance(1)))
            alternate(two(advance(2), advance(3)))
            ot = mt[4:8]
            at[0] = mark
            mhf, mhr = [k8(a) for a in take_r(4096)]
            mlr = k8(take_r(4096, mix_at)[1])
            for m in range(4):
                mt[m] = split(mhr[:, m, :], mhf[:, m, :], mlr[:, m, :], mix[:, m, :], mt[m], ot)

            def body_z(w, m):
                bk = ring.next()
                tok = gemm(bk.ap, w, hrhs, 0, None, bk.free)
                sb = tmp.next()
                tz = act(sb.ap, bk.ap, ACT.Silu, tok, sb.free)
                bk.free = [tz]
                bk2 = ring.next()
                _, tq = sq_stat(bk2, mix[:, 4 + m, :], 0, 1, ones, ot)
                r, ra, tr_ = rstd(bk2, tq, 128)
                t1 = stt(mix[:, 4 + m, :], mix[:, 4 + m, :], cc("dog"), ra, ALU.mult, ALU.mult, tr_, ot)
                r.free = [t1]
                t1 = tt(mix[:, 4 + m, :], mix[:, 4 + m, :], sb.ap, ALU.mult, t1, tz)
                sb.free = [t1]
                mt[4 + m] = split(mhr[:, 4 + m, :], mhf[:, 4 + m, :], mlr[:, 4 + m, :], mix[:, 4 + m, :], t1)
                box["t"] = tok
            for m in range(4):
                submit(piece(t["win2"][24 + m]), lambda w, m=m: body_z(w, m))
            run_waiting(0)
            for k in range(8):
                h_free[k] = [box["t"]]
            out_proj(t["wout2"], [(0, 8)], lambda k: (mhr[:, k, :], mlr[:, k, :]), mt, False, 4)
            region_free[:] = list(xtok[7])

        def peer():
            nonlocal ring
            t_pre = derived(5)
            prefetch(t["pq"][0], t["pq"][1])
            ht = pre_norm(5, t_pre)
            t_post = derived_post(5)
            at[0] = BASE
            qry = take(16 * 512).rearrange("p (k n) -> p k n", k=16)
            qt = [None] * 16
            big = take(1900)
            Sc = take(2048).rearrange("p (a n) -> p a n", a=16)
            small = take(512)
            keysm = take(256)
            iota = take(16)
            keys = keysm.rearrange("p (a n) -> p a n", a=2)
            tkeys = P.dma("sp", keysm, t["keys"], region_free)
            tiota = P.dma("sp", iota, t["iota"], region_free)
            cand = wf[:, 0:2048].rearrange("p (h n) -> p h n", h=8)
            eq = wf[:, 2048:4096]
            wfree = []
            sm_at = [0]

            def smt(n, src=small):
                a = sm_at[0]
                sm_at[0] += n
                assert sm_at[0] <= 512
                return src[:, a:a + n]
            vals = smt(256).rearrange("p (a n) -> p a n", a=16)
            bat = [0]

            def bg(n):
                a = bat[0]
                bat[0] += n
                assert bat[0] <= 1900
                return big[:, a:a + n]
            vidx = bg(256).bitcast(U32).rearrange("p (a n) -> p a n", a=16)
            vif = bg(256).rearrange("p (a n) -> p a n", a=16)
            tv = bg(128).rearrange("p (h n) -> p h n", h=8)
            tpos = bg(128).bitcast(U32).rearrange("p (h n) -> p h n", h=8)
            tab = bg(128).bitcast(U32)
            taf = bg(128)
            ea = bg(128)
            sm8 = bg(16)
            gates = [bg(128) for _ in range(2)]
            eidx = [bg(128).bitcast(U32) for _ in range(2)]
            gate_free = [[], []]
            idx_free = [[], []]
            rank = Ring(banks[4:8])
            ready = {}
            prevt = [list(region_free) + [tkeys, tiota]]

            def topk(c):
                cs = slice(128 * c, 128 * c + 128)
                last = None
                for k4 in range(4):
                    bk = rank.next()
                    for i in range(4):
                        kk = 4 * k4 + i
                        q = mm(bk.ap[:, 128 * i:128 * i + 128], [(qry[:, kk, cs], keys[:, kk % 2, :])],
                               qt[kk], tkeys, bk.free)
                    tS = act(Sc[:, 4 * k4:4 * k4 + 4, :], bk.ap.rearrange("p (a n) -> p a n", a=4), ACT.Copy, q, prevt[0])
                    bk.free = [tS]
                    for a in range(4 * k4, 4 * k4 + 4):
                        s_ = Sc[:, a, :]
                        t1 = vmax(vals[:, a, 0:8], s_, tS, prevt[0])
                        t2 = vindex(vidx[:, a, 0:8], vals[:, a, 0:8], s_, t1)
                        t3 = vdrop(s_, vals[:, a, 0:8], s_, t2)
                        t4 = vmax(vals[:, a, 8:16], s_, t3)
                        last = vindex(vidx[:, a, 8:16], vals[:, a, 8:16], s_, t4)
                        yield
                fi = vcopy(vif.rearrange("p a n -> p (a n)"), vidx.rearrange("p a n -> p (a n)"), last)
                va = vals.rearrange("p (h two) n -> p h two n", two=2)
                ia = vif.rearrange("p (h two) n -> p h two n", two=2)
                c4 = cand.rearrange("p h (a b) -> p h a b", a=16)
                t1 = tt(c4, va[:, :, 0, :].unsqueeze(3).broadcast_to([128, 8, 16, 16]),
                        va[:, :, 1, :].unsqueeze(2).broadcast_to([128, 8, 16, 16]), ALU.add, last, wfree)
                yield
                for h in range(8):
                    s_ = cand[:, h, :]
                    t2 = vmax(tv[:, h, 0:8], s_, t1)
                    t3 = vindex(tpos[:, h, 0:8], tv[:, h, 0:8], s_, t2)
                    t4 = vdrop(s_, tv[:, h, 0:8], s_, t3)
                    t5 = vmax(tv[:, h, 8:16], s_, t4)
                    last = vindex(tpos[:, h, 8:16], tv[:, h, 8:16], s_, t5)
                    yield
                posf = tpos.rearrange("p h n -> p (h n)")
                e4 = eq.rearrange("p (h k a) -> p h k a", h=8, k=16)
                iob = iota.unsqueeze(1).broadcast_to([128, 128, 16])
                t6 = fi
                for u in range(2):
                    if u == 0:
                        t1 = ts(tab, posf, 4, ALU.logical_shift_right, last)
                    else:
                        t1 = ts(tab, posf, 15, ALU.bitwise_and, t2)
                    t2 = vcopy(taf, tab, t1, t6)
                    t3 = tt(eq.rearrange("p (k a) -> p k a", a=16), taf.unsqueeze(2).broadcast_to([128, 128, 16]), iob,
                            ALU.is_equal, t2, t6, wfree)
                    yield
                    t4 = tt(e4, e4, ia[:, :, u, :].unsqueeze(2).broadcast_to([128, 8, 16, 16]), ALU.mult, t3, fi)
                    yield
                    dst = ea if u == 0 else taf
                    t6 = red(dst, eq.rearrange("p (k a) -> p k a", a=16), ALU.add, t4)
                    yield
                t7 = stt(ea, ea, 128.0, taf, ALU.mult, ALU.add, t6)
                t8 = vcopy(eidx[c % 2], ea, t7, idx_free[c % 2])
                tvb = tv[:, :, 0:1].broadcast_to([128, 8, 16])
                g3 = gates[c % 2].rearrange("p (h n) -> p h n", h=8)
                g1 = tt(g3, tv, tvb, ALU.subtract, last, gate_free[c % 2])
                g2 = act(gates[c % 2], gates[c % 2], ACT.Exp, g1)
                g4 = red(sm8[:, 0:8], g3, ALU.add, g2)
                g5 = recip(sm8[:, 8:16], sm8[:, 0:8], g4)
                g6 = tt(g3, g3, sm8[:, 8:16].unsqueeze(2).broadcast_to([128, 8, 16]), ALU.mult, g5)
                prevt[0] = [t8, g6]
                ready[c] = (t8, g6)
                yield

            first_topk = topk(0)
            ring_keep = ring
            ring = Ring(banks[0:4])
            box = {}
            for kk in range(16):
                def body(w, kk=kk):
                    bk = ring.next()
                    tok = gemm(bk.ap, w, hrhs, 0, ht, bk.free)
                    qt[kk] = act(qry[:, kk, :], bk.ap, ACT.Copy, tok, region_free)
                    if kk % 2 == 0:
                        box["b"] = ring.next()
                    bk2 = box["b"]
                    t1, tq = sq_stat(bk2, bk.ap, kk % 2, 2, ones, tok)
                    bk.free = [t1]
                    if kk % 2:
                        r, ra, tr_ = rstd(bk2, tq, 256)
                        for u in (1, 0):
                            i = kk - u
                            qt[i] = stt(qry[:, i, :], qry[:, i, :], cc("pqg", 1 - u), ra, ALU.mult, ALU.mult, tr_, qt[i])
                        r.free = [qt[kk]]
                    box["t"] = tok
                    if kk % 4 == 1 and kk > 1:
                        for _ in range(4):
                            next(first_topk)
                submit(piece(t["pq"][kk]), body)
            run_waiting(0)
            ring = ring_keep
            done = [box["t"]]
            wbase = raw_at
            wmem = arena[:, wbase:wbase + 4096]
            wfree += [x for b in raw.banks + whl.banks for x in b.free]
            gB = wf[:, 4096:5120]
            htk = take(4096).rearrange("p (c n) -> p c n", c=4)
            tht = [None] * 4
            for c in range(4):
                for k in range(8):
                    if k % 4 == 0:
                        bk = ring.next()
                    cs = slice(128 * c, 128 * c + 128)
                    q = mm(bk.ap[:, 128 * (k % 4):128 * (k % 4) + 128],
                           [(hhf[:, k, cs], ident), (hlf[:, k, cs], ident)], ht[k], bk.free)
                    if k % 4 == 3:
                        tht[c] = act(htk[:, c, 512 * (k // 4):512 * (k // 4) + 512], bk.ap, ACT.Copy, q, region_free)
                        bk.free = [tht[c]]
                if c == 0:
                    for _ in range(4):
                        next(first_topk)
            hfree = [q]
            for k in range(8):
                if k % 4 == 0:
                    bk = ring.next()
                q = mm(bk.ap[:, 128 * (k % 4):128 * (k % 4) + 128], [(post(5, k).broadcast_to([128, 128]), ident)],
                       t_post, bk.free)
                if k % 4 == 3:
                    tgB = act(gB[:, 512 * (k // 4):512 * (k // 4) + 512], bk.ap, ACT.Copy, q, wfree)
                    bk.free = [tgB]
            xtk = hf[:, 0:4096].rearrange("p (c n) -> p c n", c=4)
            txt = [None] * 4
            for c in range(4):
                for k in range(8):
                    if k % 4 == 0:
                        bk = ring.next()
                    q = tr(bk.ap[:, 128 * (k % 4):128 * (k % 4) + 128], xT[:, k, 128 * c:128 * c + 128], 128, xtok[k], bk.free)
                    if k % 4 == 3:
                        txt[c] = act(xtk[:, c, 512 * (k // 4):512 * (k // 4) + 512], bk.ap, ACT.Copy, q, hfree, done)
                        bk.free = [txt[c]]
            xfree = [q]

            hslots = []
            ringmem = [take(2048) for _ in range((WORDS - at[0]) // 2048)]
            hlo = hf[:, 4096:8192]
            for m in (hlo[:, 0:2048], hlo[:, 2048:4096]):
                hslots.append(Bank(m, P.new_sem()))
                hslots[-1].free = hfree + done
            for m in (wmem[:, 0:2048], wmem[:, 2048:4096]):
                hslots.append(Bank(m, P.new_sem()))
                hslots[-1].free = list(wfree)
            xflat = xT.rearrange("p k n -> p (k n)")
            gslots = [Bank(m, P.new_sem()) for m in ringmem]
            for g in gslots:
                g.free = list(region_free) + done
            for m in (xflat[:, 0:2048], xflat[:, 2048:4096]):
                g = Bank(m, P.new_sem())
                g.free = list(xfree)
                gslots.append(g)
            gslots += hslots
            NG = len(gslots)
            dots = [Bank(bg(GG)) for _ in range(8)]
            diag = [Bank(tmp.banks[i].ap[:, 128 * j:128 * j + 128]) for i in range(4, 8) for j in range(2)]
            for i, dgb in enumerate(diag):
                dgb.free = list(tmp.banks[4 + i // 2].free)
            for _ in first_topk:
                pass
            tv_ = t["experts"]
            n = 0
            gfin = [Bank(m) for m in (tmp.banks[0].ap, tmp.banks[1].ap, tmp.banks[2].ap, tmp.banks[3].ap)]
            for i, g in enumerate(gfin):
                g.free = list(tmp.banks[i].free)
            for c in range(4):
                tidx, tgate = ready[c]
                nxt = topk(c + 1) if c < 3 else iter(())
                acc = [banks[2 * (c % 2)], banks[2 * (c % 2) + 1]]
                for grp in range(128 // GG):
                    sl = []
                    for i in range(GG):
                        s_i = grp * GG + i
                        gs = gslots[n % NG]
                        n += 1
                        gs.uses += 1
                        P.q["pool"].append((
                            lambda e, gs=gs, s_i=s_i, c=c: e.indirect_dma_start(
                                out=gs.ap, out_offset=None, in_=tv_,
                                in_offset=bass.IndirectOffsetOnAxis(ap=eidx[c % 2][:, s_i:s_i + 1], axis=0)),
                            [tidx] + gs.free, gs.sem, 16))
                        tg = (gs.sem, 16 * gs.uses)
                        dt_ = dots[grp % 8]
                        t1 = put("dve", lambda e, gs=gs, i=i, dt_=dt_, c=c: e.tensor_tensor_reduce(
                            gs.ap[:, 0:1024], gs.ap[:, 0:1024], htk[:, c, :], 1.0, 0.0, ALU.mult, ALU.add,
                            dt_.ap[:, i:i + 1]), tg, tht[c], dt_.free if i == 0 else None)
                        sl.append((gs, tg, t1))
                    dt_ = dots[grp % 8]
                    t2 = act(dt_.ap, dt_.ap, ACT.Gelu, t1)
                    t3 = tt(dt_.ap, dt_.ap, gates[c % 2][:, grp * GG:grp * GG + GG], ALU.mult, t2, tgate)
                    for i in range(GG):
                        s_i = grp * GG + i
                        gs, tg, t1 = sl[i]
                        dg = diag[(grp * GG + i) % 8]
                        t4 = act(dg.ap, ident, ACT.Copy, t3, dg.free, scale=dt_.ap[:, i:i + 1])
                        for u in range(2):
                            q = mm(acc[u].ap, [(dg.ap, gs.ap[:, 1024 + 512 * u:1536 + 512 * u])], t4, tg,
                                   acc[u].free if s_i == 0 else None, start=s_i == 0, stop=s_i == 127)
                        dg.free = [q]
                        gs.free = [q, t1]
                    dt_.free = [t4]
                    next(nxt, None)
                idx_free[c % 2] = [gs.free[0]]
                gate_free[c % 2] = [t3]
                for _ in nxt:
                    pass
                for u in range(2):
                    f = gfin[2 * (c % 2) + u]
                    us = slice(512 * u, 512 * u + 512)
                    t5 = tt(f.ap, acc[u].ap, gB[:, us], ALU.mult, q, tgB, f.free)
                    acc[u].free = [t5]
                    t6 = tt(f.ap, f.ap, xtk[:, c, us], ALU.add, t5, txt[c])
                    tk = P.dma("sp", out[0, 128 * c:128 * c + 128, us], f.ap, t6, store=True)
                    f.free = [tk]

        conv_mixer()
        ffn(0, 1)
        ssd_mixer()
        ffn(1, 3)
        hybrid()
        peer()

        block = ctx.enter_context(nc.Block())

        @block.sync
        def _(e):
            P.replay("sp", e)
            for s, v in P.stores:
                e.wait_ge(s, v)

        @block.gpsimd
        def _(e):
            P.replay("pool", e)

        @block.scalar
        def _(e):
            P.replay("act", e)

        @block.tensor
        def _(e):
            P.replay("pe", e)

        @block.vector
        def _(e):
            P.replay("dve", e)


def _layout(inputs):
    import numpy as np

    g = {k: np.asarray(v) for k, v in inputs.items()}

    def slabs(w, width=128):
        k, n = w.shape
        return np.ascontiguousarray(
            w.reshape(k // 128, 128, n // width, width).transpose(2, 1, 0, 3).reshape(n // width, 128, -1))

    def colv(v):
        return v.reshape(-1, 128).T

    a = {}
    a["xT"] = np.ascontiguousarray(g["x"][0].reshape(S, 8, 128).transpose(2, 1, 0).reshape(128, -1))
    a["ada"] = slabs(g["ada_w"], 512)
    a["ada2"] = slabs(g["w_ada_2"][0], 512)
    w = g["a_w_in"][0]
    a["ain"] = slabs(np.concatenate([w[:, 1024:2048], w[:, 2048:3072], w[:, 0:1024]], axis=1))
    a["aout"] = slabs(g["a_w_out"][0])
    w = g["m_w_in"][0]
    a["mdt"] = slabs(np.pad(w[:, 6144:6176], ((0, 0), (0, 96))))[0]
    a["mxbc"] = slabs(np.concatenate([w[:, 4096:5120], w[:, 5120:6144], w[:, 2048:4096]], axis=1))
    a["mz"] = slabs(w[:, 0:2048])
    a["mout"] = slabs(g["m_w_out"][0])
    fi = []
    fo = []
    for i in range(2):
        w = g["f_w_in"][i]
        w = np.concatenate([w[:, 0:FF].reshape(D, KF, 128), w[:, FF:2 * FF].reshape(D, KF, 128)], axis=2)
        fi.append(slabs(w.reshape(D, 2 * FF)))
        fo.append(slabs(g["f_w_out"][i]))
    a["fin"] = np.stack(fi)
    a["fout"] = np.stack(fo)
    w = g["w_in_2"][0]
    a["win2"] = slabs(w[:, 0:3584])
    ba = np.zeros((D, 128), np.float32)
    ba[:, 0:4] = w[:, 3584:3588]
    ba[:, 32:36] = w[:, 3588:3592]
    a["win2ba"] = slabs(ba)[0]
    a["wout2"] = slabs(g["w_out_2"][0])
    a["pq"] = slabs(g["peer_w_query_2"][0])
    a["keys"] = np.ascontiguousarray(np.concatenate(
        [g["peer_sub_keys_1_2"][0].T, g["peer_sub_keys_2_2"][0].T], axis=1))
    a["iota"] = np.ascontiguousarray(np.broadcast_to(np.arange(16, dtype=np.float32), (128, 16)))
    a["experts"] = np.concatenate([g["peer_expert_down_2"][0], g["peer_expert_up_2"][0]], axis=1)
    d = 384 + np.arange(128)[:, None] - np.arange(512)[None, :]
    idx = np.clip(d, -128, 128) + 128
    a["relT"] = np.ascontiguousarray(g["attn_rel_bias_2"][0][:, idx].transpose(1, 0, 2).reshape(128, -1))

    col = np.zeros((128, NCOL), np.float32)

    def place(name, v):
        v = v if v.ndim == 2 else v[:, None]
        col[:v.shape[0], COL[name]:COL[name] + v.shape[1]] = v

    place("c", colv(g["c"][0]))
    place("adab", colv(g["ada_b"]))
    place("ng", colv(g["norm_g"].reshape(-1)))
    place("acw", colv(g["a_conv_w"][0].reshape(-1)))
    place("mcw", colv(g["m_conv_w"][0].reshape(-1)))
    place("mcb", colv(g["m_conv_b"][0]))
    place("mng", colv(g["m_norm_g"][0]))
    place("md", colv(np.repeat(g["m_d"][0], 64)))
    place("c2", colv(g["c_2"][0]))
    place("adab2", colv(g["b_ada_2"][0]))
    place("n1", colv(g["norm1_gain_2"][0]))
    place("n2", colv(g["norm2_gain_2"][0]))
    place("aog", colv(g["attn_out_gain_2"][0]))
    place("qg", np.tile(g["attn_q_gain_2"][0], 2))
    place("kg", np.tile(g["attn_k_gain_2"][0], 2))
    place("dcw", colv(g["dn_conv_w_2"][0].reshape(-1)))
    place("dog", g["dn_out_gain_2"][0])
    place("pqg", colv(g["peer_query_gain_2"][0]))
    place("mdt", g["m_dt_bias"][0])
    place("mal", g["m_a_log"][0])
    place("dal", np.pad(g["dn_a_log_2"][0], (32, 0)))
    place("ddt", np.pad(g["dn_dt_bias_2"][0], (32, 0)))
    a["cols"] = col

    def stack(ms):
        return np.ascontiguousarray(np.stack(ms, 1).reshape(128, -1).astype(np.float32))

    i, j = np.arange(128)[:, None], np.arange(128)[None, :]
    cs = [i == j, i <= j, i < j, i // 64 == j // 64, (i >= 0) & (j >= 0), i > j]
    a["consts"] = stack(cs)
    a["levels"] = stack([(i // (2 * b) == j // (2 * b)) & ((i // b) % 2 == 1) & ((j // b) % 2 == 0) for b in LEVELS])
    return a


def kernel(**inputs):
    import numpy as _np
    import concourse.bacc as _bacc
    from concourse import mybir as _mybir
    from concourse.bass_utils import run_bass_kernel_spmd as _run

    nc = _bacc.Bacc("TRN2", target_bir_lowering=False, num_devices=1)
    arrays = {"in_" + k: v for k, v in _layout(inputs).items()}
    aps = {k: nc.dram_tensor("in_" + k, arrays["in_" + k].shape, _mybir.dt.float32, kind="ExternalInput").ap()
           for k in (n[3:] for n in arrays)}
    out = nc.dram_tensor("out", (1, S, D), _mybir.dt.float32, kind="ExternalOutput").ap()
    build(nc, aps, out)
    r = _run(nc, [arrays], core_ids=[0])
    return r.results[0]["out"]
```
